# Optimizing a Trainium2 kernel written in Bass

```python
import jax, jax.numpy as jnp
from jax import lax
import numpy as np

D_MODEL = 2048
BATCH = 1
SEQ = 256
DEPTH = 2

D_MIX = D_MODEL
GROUP_W = D_MIX // 4
EPS = 1e-6
ROPE_THETA = 10000.0

RET_HEADS = 4
RET_HD = GROUP_W // RET_HEADS
RET_CHUNK = 128

GLA_HEADS = 4
GLA_DK = GROUP_W // 2 // GLA_HEADS
GLA_DV = GROUP_W // GLA_HEADS
GLA_GATE_RANK = 16
GLA_TAU = 16.0
GLA_CHUNK = 64

POOL_GROUPS = 4
POOL_GW = GROUP_W // POOL_GROUPS
POOL_WINDOWS = (2, 4, 8, 16)

MLA_HEADS = 4
MLA_NOPE = 128
MLA_ROPE = 64
MLA_V = GROUP_W // MLA_HEADS
MLA_Q_RANK = D_MODEL // 4
MLA_KV_RANK = D_MODEL // 8
MLA_QBLOCK = 128

SPLIT_SIZES = (
    GROUP_W, GROUP_W, GROUP_W, GROUP_W,
    GLA_HEADS * GLA_DK, GLA_HEADS * GLA_DK, GROUP_W, GROUP_W,
    GLA_GATE_RANK, GLA_GATE_RANK,
    GROUP_W, GROUP_W,
    MLA_Q_RANK, MLA_KV_RANK, MLA_ROPE, GROUP_W,
)
IN_COLS = sum(SPLIT_SIZES)

kernel_name = "bidir_hybrid_headgroup_block"

def _rmsnorm(x, g):
    xf = x.astype(jnp.float32)
    y = xf * lax.rsqrt(jnp.mean(xf * xf, axis=-1, keepdims=True) + EPS)
    return y * g.astype(jnp.float32)

def _rope_tables(dim, s):
    inv = 1.0 / (ROPE_THETA ** (jnp.arange(0, dim, 2, dtype=jnp.float32) / dim))
    ang = jnp.arange(s, dtype=jnp.float32)[:, None] * inv[None, :]
    return jnp.cos(ang), jnp.sin(ang)

def _rotate(x, cos, sin):
    half = x.shape[-1] // 2
    x1, x2 = x[..., :half], x[..., half:]
    return jnp.concatenate([x1 * cos - x2 * sin, x2 * cos + x1 * sin], axis=-1)

def _heads(t, h, d):
    b, s, _ = t.shape
    return t.reshape(b, s, h, d).transpose(0, 2, 1, 3)

def _head_rmsnorm(o, g):
    b, h, s, d = o.shape
    t = _rmsnorm(o.transpose(0, 2, 1, 3), g.reshape(h, d))
    return t.reshape(b, s, h * d)

def _retention_scan(q, k, v, gamma):
    b, h, s, dk = q.shape
    dv = v.shape[-1]
    c = RET_CHUNK
    n = s // c
    q = q.reshape(b, h, n, c, dk)
    k = k.reshape(b, h, n, c, dk)
    v = v.reshape(b, h, n, c, dv)
    log_g = jnp.log(gamma)
    idx = jnp.arange(c, dtype=jnp.float32)
    diff = idx[:, None] - idx[None, :]
    dmat = jnp.where(diff >= 0, jnp.exp(jnp.maximum(diff, 0.0)[None] * log_g[:, None, None]), 0.0)
    scores = jnp.einsum('bhnid,bhnjd->bhnij', q, k) * dmat[None, :, None]
    o_inner = jnp.einsum('bhnij,bhnje->bhnie', scores, v)
    k_dec = k * jnp.exp((c - 1 - idx)[None, :] * log_g[:, None])[None, :, None, :, None]
    kv = jnp.einsum('bhncd,bhnce->bhnde', k_dec, v)
    chunk_decay = jnp.exp(c * log_g)[:, None, None]

    def step(state, kv_n):
        return chunk_decay * state + kv_n, state

    _, s_before = lax.scan(step, jnp.zeros((b, h, dk, dv), jnp.float32), jnp.moveaxis(kv, 2, 0))
    s_before = jnp.moveaxis(s_before, 0, 2)
    q_dec = q * jnp.exp((idx + 1.0)[None, :] * log_g[:, None])[None, :, None, :, None]
    o_cross = jnp.einsum('bhncd,bhnde->bhnce', q_dec, s_before)
    return (o_inner + o_cross).reshape(b, h, s, dv)

def _gla_scan(q, k, v, log_a):
    b, h, s, dk = q.shape
    dv = v.shape[-1]
    c = GLA_CHUNK
    n = s // c
    q = q.reshape(b, h, n, c, dk)
    k = k.reshape(b, h, n, c, dk)
    v = v.reshape(b, h, n, c, dv)
    cum = jnp.cumsum(log_a.reshape(b, h, n, c, dk), axis=3)
    q_t = q * jnp.exp(cum)
    k_t = k * jnp.exp(-cum)
    mask = jnp.tril(jnp.ones((c, c), dtype=bool))
    scores = jnp.where(mask, jnp.einsum('bhnid,bhnjd->bhnij', q_t, k_t), 0.0)
    o_inner = jnp.einsum('bhnij,bhnje->bhnie', scores, v)
    last = cum[..., -1:, :]
    kv = jnp.einsum('bhncd,bhnce->bhnde', k * jnp.exp(last - cum), v)
    decay = jnp.exp(last[..., 0, :])

    def step(state, inp):
        kv_n, d_n = inp
        return d_n[..., None] * state + kv_n, state

    _, s_before = lax.scan(step, jnp.zeros((b, h, dk, dv), jnp.float32),
                           (jnp.moveaxis(kv, 2, 0), jnp.moveaxis(decay, 2, 0)))
    s_before = jnp.moveaxis(s_before, 0, 2)
    o_cross = jnp.einsum('bhncd,bhnde->bhnce', q_t, s_before)
    return (o_inner + o_cross).reshape(b, h, s, dv)

def _retention_branch(q, k, v, gate, norm_g, cos, sin):
    qh = _rotate(_heads(q, RET_HEADS, RET_HD), cos, sin)
    kh = _rotate(_heads(k, RET_HEADS, RET_HD), cos, sin) * (RET_HD ** -0.5)
    vh = _heads(v, RET_HEADS, RET_HD)
    gamma_f = 1.0 - 2.0 ** (-5.0 - jnp.arange(RET_HEADS, dtype=jnp.float32))
    gamma_b = gamma_f[::-1]
    o_f = _retention_scan(qh, kh, vh, gamma_f)
    o_b = jnp.flip(_retention_scan(jnp.flip(qh, 2), jnp.flip(kh, 2), jnp.flip(vh, 2), gamma_b), 2)
    return jax.nn.silu(gate) * _head_rmsnorm(o_f + o_b, norm_g)

def _gla_branch(q, k, v, gate, a_f, a_b, wa2_f, ba_f, wa2_b, ba_b, norm_g):
    qh = _heads(q, GLA_HEADS, GLA_DK) * (GLA_DK ** -0.5)
    kh = _heads(k, GLA_HEADS, GLA_DK)
    vh = _heads(v, GLA_HEADS, GLA_DV)
    la_f = _heads(jax.nn.log_sigmoid(a_f @ wa2_f + ba_f) / GLA_TAU, GLA_HEADS, GLA_DK)
    la_b = _heads(jax.nn.log_sigmoid(a_b @ wa2_b + ba_b) / GLA_TAU, GLA_HEADS, GLA_DK)
    o_f = _gla_scan(qh, kh, vh, la_f)
    o_b = jnp.flip(_gla_scan(jnp.flip(qh, 2), jnp.flip(kh, 2), jnp.flip(vh, 2), jnp.flip(la_b, 2)), 2)
    return jax.nn.silu(gate) * _head_rmsnorm(o_f + o_b, norm_g)

def _pool_branch(u, gate, pool_w, pool_scale):
    b, s, _ = u.shape
    ug = u.reshape(b, s, POOL_GROUPS, POOL_GW)
    cs = jnp.concatenate([jnp.zeros((b, 1, POOL_GROUPS, POOL_GW), jnp.float32),
                          jnp.cumsum(ug, axis=1)], axis=1)
    t = jnp.arange(s)
    outs = []
    for g, w_len in enumerate(POOL_WINDOWS):
        lo = jnp.clip(t - w_len // 2, 0, s)
        hi = jnp.clip(t + w_len // 2, 0, s)
        csg = cs[:, :, g]
        win_sum = jnp.take(csg, hi, axis=1) - jnp.take(csg, lo, axis=1)
        cnt = (hi - lo).astype(jnp.float32)[None, :, None]
        outs.append(win_sum / cnt - ug[:, :, g])
    pooled = jnp.stack(outs, axis=2)
    mixed = jnp.einsum('bsgc,gcd->bsgd', pooled, pool_w).reshape(b, s, GROUP_W)
    return jax.nn.silu(gate) * (mixed * pool_scale)

def _mla_branch(q_lat, kv_lat, k_pe, gate, q_norm_g, wq_b, kv_norm_g, wkv_b, qn_g, kn_g, cos, sin):
    b, s, _ = q_lat.shape
    q = (_rmsnorm(q_lat, q_norm_g) @ wq_b).reshape(b, s, MLA_HEADS, MLA_NOPE + MLA_ROPE)
    kv = (_rmsnorm(kv_lat, kv_norm_g) @ wkv_b).reshape(b, s, MLA_HEADS, MLA_NOPE + MLA_V)
    k_nope, v = kv[..., :MLA_NOPE], kv[..., MLA_NOPE:]
    k = jnp.concatenate([k_nope, jnp.broadcast_to(k_pe[:, :, None, :], (b, s, MLA_HEADS, MLA_ROPE))], axis=-1)
    q = _rmsnorm(q, qn_g)
    k = _rmsnorm(k, kn_g)
    c, sn = cos[:, None, :], sin[:, None, :]
    q = jnp.concatenate([q[..., :MLA_NOPE], _rotate(q[..., MLA_NOPE:], c, sn)], axis=-1)
    k = jnp.concatenate([k[..., :MLA_NOPE], _rotate(k[..., MLA_NOPE:], c, sn)], axis=-1)
    q = q.transpose(0, 2, 1, 3)
    k = k.transpose(0, 2, 1, 3)
    v = v.transpose(0, 2, 1, 3)
    scale = (MLA_NOPE + MLA_ROPE) ** -0.5
    nb = s // MLA_QBLOCK
    qb = q.reshape(b, MLA_HEADS, nb, MLA_QBLOCK, MLA_NOPE + MLA_ROPE).transpose(2, 0, 1, 3, 4)

    def attend(q_blk):
        sc = jnp.einsum('bhqd,bhkd->bhqk', q_blk, k).astype(jnp.float32) * scale
        p = jax.nn.softmax(sc, axis=-1)
        return jnp.einsum('bhqk,bhkd->bhqd', p, v)

    o = lax.map(attend, qb)
    o = o.transpose(1, 0, 3, 2, 4).reshape(b, s, MLA_HEADS * MLA_V)
    return jax.nn.silu(gate) * o

def setup_inputs(seed: int = 0) -> dict:
    key = jax.random.key(seed)
    ks = jax.random.split(key, 20)
    f32 = jnp.float32

    def nrm(k, shape, scale):
        return jax.random.normal(k, shape, f32) * scale

    def gain(k, shape):
        return 1.0 + 0.02 * jax.random.normal(k, shape, f32)

    return {
        "x": jax.random.normal(ks[0], (BATCH, SEQ, D_MODEL), f32),
        "norm_g": gain(ks[1], (DEPTH, D_MODEL)),
        "w_in": nrm(ks[2], (DEPTH, D_MODEL, IN_COLS), D_MODEL ** -0.5),
        "ret_norm_g": gain(ks[3], (DEPTH, GROUP_W)),
        "gla_wa2_f": nrm(ks[4], (DEPTH, GLA_GATE_RANK, GLA_HEADS * GLA_DK), GLA_GATE_RANK ** -0.5),
        "gla_ba_f": nrm(ks[5], (DEPTH, GLA_HEADS * GLA_DK), 0.1),
        "gla_wa2_b": nrm(ks[6], (DEPTH, GLA_GATE_RANK, GLA_HEADS * GLA_DK), GLA_GATE_RANK ** -0.5),
        "gla_ba_b": nrm(ks[7], (DEPTH, GLA_HEADS * GLA_DK), 0.1),
        "gla_norm_g": gain(ks[8], (DEPTH, GROUP_W)),
        "pool_w": nrm(ks[9], (DEPTH, POOL_GROUPS, POOL_GW, POOL_GW), POOL_GW ** -0.5),
        "pool_scale": gain(ks[10], (DEPTH, GROUP_W)),
        "mla_q_norm_g": gain(ks[11], (DEPTH, MLA_Q_RANK)),
        "mla_wq_b": nrm(ks[12], (DEPTH, MLA_Q_RANK, MLA_HEADS * (MLA_NOPE + MLA_ROPE)), MLA_Q_RANK ** -0.5),
        "mla_kv_norm_g": gain(ks[13], (DEPTH, MLA_KV_RANK)),
        "mla_wkv_b": nrm(ks[14], (DEPTH, MLA_KV_RANK, MLA_HEADS * (MLA_NOPE + MLA_V)), MLA_KV_RANK ** -0.5),
        "mla_qk_norm_q": gain(ks[15], (DEPTH, MLA_NOPE + MLA_ROPE)),
        "mla_qk_norm_k": gain(ks[16], (DEPTH, MLA_NOPE + MLA_ROPE)),
        "w_out": nrm(ks[17], (DEPTH, D_MIX, D_MODEL), D_MIX ** -0.5),
    }

def reference(x, norm_g, w_in, ret_norm_g, gla_wa2_f, gla_ba_f, gla_wa2_b, gla_ba_b, gla_norm_g,
              pool_w, pool_scale, mla_q_norm_g, mla_wq_b, mla_kv_norm_g, mla_wkv_b,
              mla_qk_norm_q, mla_qk_norm_k, w_out):
    s = x.shape[1]
    cos_r, sin_r = _rope_tables(RET_HD, s)
    cos_m, sin_m = _rope_tables(MLA_ROPE, s)
    points = [int(p) for p in np.cumsum(SPLIT_SIZES)[:-1]]
    for l in range(DEPTH):
        h = _rmsnorm(x, norm_g[l]).astype(x.dtype)
        z = (h @ w_in[l]).astype(jnp.float32)
        (rq, rk, rv, rg, gq, gk, gv, gg, ga_f, ga_b, pv, pg, mq, mkv, mkr, mg) = jnp.split(z, points, axis=-1)
        y_a = _retention_branch(rq, rk, rv, rg, ret_norm_g[l], cos_r, sin_r)
        y_b = _gla_branch(gq, gk, gv, gg, ga_f, ga_b, gla_wa2_f[l], gla_ba_f[l],
                          gla_wa2_b[l], gla_ba_b[l], gla_norm_g[l])
        y_c = _pool_branch(pv, pg, pool_w[l], pool_scale[l])
        y_d = _mla_branch(mq, mkv, mkr, mg, mla_q_norm_g[l], mla_wq_b[l], mla_kv_norm_g[l], mla_wkv_b[l],
                          mla_qk_norm_q[l], mla_qk_norm_k[l], cos_m, sin_m)
        y = jnp.concatenate([y_a, y_b, y_c, y_d], axis=-1).astype(x.dtype)
        x = x + y @ w_out[l]
    return x


_drawn_inputs = setup_inputs


def setup_inputs(seed=0):
    import zlib

    import numpy as np

    out = dict(_drawn_inputs(seed))
    spreads = {}
    factors = {'ret_norm_g': 7.433,
     'gla_ba_f': 4.872,
     'gla_ba_b': 4.912,
     'gla_norm_g': 7.328,
     'pool_scale': 8.0,
     'mla_q_norm_g': 8.0,
     'mla_kv_norm_g': 8.0,
     'mla_qk_norm_q': 8.0,
     'mla_qk_norm_k': 8.0}
    for name, (base, spread) in spreads.items():
        noise = np.random.default_rng([zlib.crc32(name.encode()), seed]).standard_normal(out[name].shape)
        drawn = base * np.exp(spread * noise) if base else spread * noise
        out[name] = __import__('jax').numpy.asarray(drawn.astype(out[name].dtype))
    for name, factor in factors.items():
        out[name] = (out[name] * factor).astype(out[name].dtype)
    return out
```

```python
from contextlib import ExitStack

import concourse.bass as bass
from concourse import mybir

F32 = mybir.dt.float32
F32R = mybir.dt.float32r
I32 = mybir.dt.int32
ALU = mybir.AluOpType
ACT = mybir.ActivationFunctionType
AX_X = mybir.AxisListType.X

P = 128
D_MODEL, SEQ, DEPTH = 2048, 256, 2
MT = SEQ // P
KT = D_MODEL // P
GROUP_W = D_MODEL // 4
HEADS = 4
HD = GROUP_W // HEADS
GT = GROUP_W // P
EPS = 1e-6
GLA_DK, GLA_RANK, GLA_TAU, GLA_CHUNK = 64, 16, 16.0, 64
POOL_WINDOWS = (2, 4, 8, 16)
POOL_REACH = P + max(POOL_WINDOWS) // 2
NOPE, ROPE, Q_RANK, KV_RANK = 128, 64, 512, 256
QK_W = NOPE + ROPE
LAT_W = KV_RANK + 2 * GLA_RANK + ROPE
WA_ROW = 32

RING = 4
GRAN = 2 * 512

SLOT = {"D": 0, "C": GT, "B": 2 * GT, "A": 3 * GT}

STAGES = (
    [("mq", 512, "x", 0, KT, 2), ("lat", LAT_W, "x", 0, KT, 2), ("mg", 512, "x", 0, KT, 2)]
    + [(f"wq{i}", 2 * QK_W, "y", SLOT["B"], Q_RANK // P, 2) for i in range(2)]
    + [(f"wkv{i}", 512, "y", SLOT["A"], KV_RANK // P, 1) for i in range(2)]
    + [(n, 512, "x", 0, KT, 2) for n in ("pv", "pg", "gqk", "gv", "gg", "rq", "rk", "rv", "rg")]
    + [(f"out{i}", 512, "y", 0, KT, 2) for i in range(4)]
)
PLAN = []
END = {}
for s_, (n_, w_, t_, b_, k_, per_) in enumerate(STAGES):
    for q_ in range(k_ // per_):
        PLAN.append((s_, [b_ + per_ * q_ + i_ for i_ in range(per_)]))
    END[n_] = len(PLAN)
GRANULES = len(PLAN)
PER_RING = GRANULES // RING
assert GRANULES % RING == 0 and len(STAGES) % 2 == 0
STAGE_OF = {n_: s_ for s_, (n_, *_) in enumerate(STAGES)}

CONSTS, nc_ = {}, 0
for n_, w_ in (("ident", P), ("tri_f", P), ("tri_b", P), ("after", P), ("before", P),
               ("decay", HEADS * 3 * P), ("rcos", MT * HD // 2), ("rsin", MT * HD // 2),
               ("mcos", MT * ROPE // 2), ("msin", MT * ROPE // 2), ("mnsin", MT * ROPE // 2),
               ("band", 4 * MT * POOL_REACH)):
    CONSTS[n_] = (nc_, w_)
    nc_ += w_
CONST_W = nc_
G_NORM, G_Y, G_QN, G_KVN, G_QK = 0, KT, 2 * KT, 2 * KT + 4, 2 * KT + 6
GAIN_W = 2 * KT + 8
M_POOL, M_WA, M_ROPE = 0, GROUP_W, 2 * GROUP_W
MAT_W = 2 * GROUP_W + 2 * ROPE


class Signal:

    def __init__(self, sem, per_layer, primed):
        self.sem, self.per_layer, self.primed = sem, per_layer, primed

    def at(self, l, n):
        return self.sem, l * self.per_layer + (n + self.primed)


def build(nc, x_in, stream, mats_in, gains_in, consts_in, out):
    with ExitStack() as ctx:
        def sb(name, shape, dt=F32):
            return ctx.enter_context(nc.sbuf_tensor(name, shape, dt))

        def signal(name, per_layer, primed=0):
            return Signal(ctx.enter_context(nc.semaphore(name)), per_layer, primed)

        raw = [sb(f"raw{r}", [P, GRAN]) for r in range(RING)]
        hi = [sb(f"hi{r}", [P, GRAN], F32R) for r in range(RING)]
        lo = [sb(f"lo{r}", [P, GRAN], F32R) for r in range(RING)]
        xT_hi = sb("xT_hi", [P, KT, SEQ], F32R)
        xT_lo = sb("xT_lo", [P, KT, SEQ], F32R)
        yT_hi = sb("yT_hi", [P, KT, SEQ], F32R)
        yT_lo = sb("yT_lo", [P, KT, SEQ], F32R)
        x = sb("x", [P, MT, D_MODEL])
        consts = sb("consts", [P, CONST_W])
        gains_all = sb("gains_all", [P, DEPTH * GAIN_W])
        gains = sb("gains", [P, GAIN_W])
        mats = sb("mats", [P, MAT_W])
        rope_tab = sb("rope_tab", [P, 2, 2, MT, ROPE])
        gate0 = sb("gate0", [P, MT, GROUP_W])
        gate1 = sb("gate1", [P, MT, GROUP_W])
        aT = sb("aT", [P, MT, P])
        q_heads = sb("q_heads", [P, 2, 2, 2, SEQ])
        k_dec = sb("k_dec", [P, 2, 2, 2 * P])
        keep_bits = sb("keep_bits", [P, 2, P], I32)
        work = sb("work", [P, 8448])
        stat = sb("stat", [P, 64])

        def const(name):
            at, w = CONSTS[name]
            return consts[:, at:at + w]

        def area(at, width, pattern=None, **sizes):
            v = work[:, at:at + width]
            return v.rearrange(pattern, **sizes) if pattern else v

        zq = area(0, 1024, "p (m c) -> p m c", m=MT)
        zlat = area(1024, MT * LAT_W, "p (m c) -> p m c", m=MT)
        qr = area(1792, 512, "p (m h c) -> p m h c", m=MT, h=HEADS)
        q_sb = area(2304, 1536, "p (m h c) -> p m h c", m=MT, h=HEADS)
        probs = area(1792, 2048, "p (m h j) -> p m h j", m=MT, h=HEADS)
        kv_sb = area(3840, 2048, "p (m h c) -> p m h c", m=MT, h=HEADS)
        kr = area(5888, 512, "p (m h c) -> p m h c", m=MT, h=HEADS)
        sq_d = area(0, 768)
        rot_d = area(0, 512, "p (m h c) -> p m h c", m=MT, h=HEADS)
        kpe = area(768, 128, "p (m c) -> p m c", m=MT)
        kpe_x = area(896, 128, "p (m c) -> p m c", m=MT)
        krT = area(0, 512, "p (a t) -> p a t", a=2)
        probsT = area(512, 1024, "p (b j t) -> p b j t", b=2, j=MT)
        u = area(6400, 1024, "p (m c) -> p m c", m=MT)
        pooledT = area(7424, 1024, "p (g t) -> p g t", g=4)
        zb = area(0, 1024, "p (m a c) -> p m a c", m=MT, a=2)
        v_b = area(1024, 1024, "p (m c) -> p m c", m=MT)
        la = area(2048, 1024, "p (m c) -> p m c", m=MT)
        score_b = area(2048, 1024, "p (m h i) -> p m h i", m=MT, h=HEADS)
        e_pos = area(3072, 1024, "p (d f t) -> p d f t", d=2, f=2)
        e_neg = area(4096, 1024, "p (d f t) -> p d f t", d=2, f=2)
        sq_b = area(4096, 512)
        e_rem = area(5120, 1024, "p (m d c) -> p m d c", m=MT, d=2)
        picked = area(7680, 512, "p (h i) -> p h i", h=HEADS)
        state = area(6144, 1536, "p (d n a e) -> p d n a e", d=2, n=3, a=2)
        rq_rot = area(0, 1024, "p (n c) -> p n c", n=MT * HEADS)
        rk_rot = area(1024, 1024, "p (n c) -> p n c", n=MT * HEADS)
        score_a = area(0, 2048, "p (h j t) -> p h j t", h=HEADS, j=MT)
        qT_a = area(2048, 1024, "p (h t) -> p h t", h=HEADS)
        rot_a = area(3072, 1024, "p (n c) -> p n c", n=MT * HEADS)
        sq_a = area(3072, 512)
        kT_a = area(4096, 1024, "p (h t) -> p h t", h=HEADS)
        z_rk = area(5120, 1024, "p (m c) -> p m c", m=MT)
        v_a = area(6144, 1024, "p (m c) -> p m c", m=MT)

        cols, cols_d = iter(range(64)), iter(range(1728, 1792))

        def stats(n):
            at = [next(cols) for _ in range(n)][0]
            return stat[:, at:at + n]

        def stats_d(n):
            at = [next(cols_d) for _ in range(n)][0]
            return work[:, at:at + n]

        x_sq = stats(MT * 4).rearrange("p (m c) -> p m c", m=MT)
        x_ms, x_rs = stats(MT), stats(MT)
        lq_sq, lq_ms, lq_rs = stats(MT), stats(MT), stats(MT)
        lk_sq, lk_ms, lk_rs, kpe_sq = stats(MT), stats(MT), stats(MT), stats(MT)
        q_sq, q_rs, k_sq, k_rs = stats_d(8), stats_d(8), stats_d(8), stats_d(8)
        q_ms, k_ms = q_sq, k_sq
        top, neg_top, p_sum, p_inv = stats_d(8), stats_d(8), stats_d(8), stats_d(8)
        o_sq, o_ms, o_rs = stats(8), stats(8), stats(8)
        minus_half = stats(8)

        pair = [[ctx.enter_context(nc.psum_tensor(f"pair{a}{m}", [P, 512], F32)) for m in range(MT)]
                for a in range(2)]
        bank = [ctx.enter_context(nc.psum_tensor(f"bank{b}", [P, 512], F32)) for b in range(4)]

        loaded = [signal(f"loaded{r}", 16 * PER_RING) for r in range(RING)]
        rounded = [signal(f"rounded{r}", PER_RING) for r in range(RING)]
        split = [signal(f"split{r}", PER_RING, primed=1) for r in range(RING)]
        multiplied = [signal(f"multiplied{r}", PER_RING, primed=1) for r in range(RING)]
        taken = [signal(f"taken{a}", len(STAGES), primed=1) for a in range(2)]
        x_loaded = [signal(f"x_loaded{c}", 0) for c in range(4)]
        ident_loaded = signal("ident_loaded", 0)
        gains_loaded = signal("gains_loaded", 0)
        consts_loaded = signal("consts_loaded", 0)
        mats_loaded = signal("mats_loaded", 16)
        stored = signal("stored", 0)
        cleared = signal("cleared", 0)
        bits_ready = signal("bits_ready", 2)
        added = [signal(f"added{c}", MT, primed=1) for c in range(4)]
        gains_ready = signal("gains_ready", 1)
        act_step = signal("act_step", 4)
        dve_step = signal("dve_step", 24)
        pool_step = signal("pool_step", 0)
        tabs_ready = signal("tabs_ready", 6)
        x_filled, xT_rounded, xT_ready = signal("x_filled", 8), signal("xT_rounded", KT), signal("xT_ready", KT)
        x_squared, x_ms_ready, x_rs_ready = signal("x_squared", 8), signal("x_ms_ready", 1), signal("x_rs_ready", 1)
        zq_ready, zlat_ready = signal("zq_ready", MT), signal("zlat_ready", MT)
        lq_squared, lq_ms_ready, lq_rs_ready = signal("lq_squared", MT), signal("lq_ms_ready", 1), signal("lq_rs_ready", 1)
        lk_squared, lk_ms_ready, lk_rs_ready = signal("lk_squared", 2 * MT), signal("lk_ms_ready", 1), signal("lk_rs_ready", 1)
        lq_filled, lqT_rounded, lqT_ready = signal("lq_filled", 2), signal("lqT_rounded", 4), signal("lqT_ready", 4)
        lk_filled, lkT_rounded, lkT_ready = signal("lk_filled", 1), signal("lkT_rounded", 2), signal("lkT_ready", 2)
        aT_filled, aT_ready = signal("aT_filled", 1), signal("aT_ready", 1)
        gate0_ready, gate1_ready = signal("gate0_ready", 2 * MT), signal("gate1_ready", 2 * MT)
        q_ready, kv_ready = signal("q_ready", 2 * MT), signal("kv_ready", 2 * MT)
        q_squared, q_ms_ready, q_rs_ready = signal("q_squared", MT), signal("q_ms_ready", 1), signal("q_rs_ready", 1)
        k_squared, k_ms_ready, k_rs_ready = signal("k_squared", MT), signal("k_ms_ready", 1), signal("k_rs_ready", 1)
        q_sq_read = signal("q_sq_read", 4)
        ob_sq_read, oa_sq_read = signal("ob_sq_read", 2), signal("oa_sq_read", 2)
        q_scaled, k_scaled = signal("q_scaled", 1), signal("k_scaled", 1)
        q_turned, k_turned = signal("q_turned", 1), signal("k_turned", 1)
        tq_filled, qT_rounded, qT_ready = signal("tq_filled", 2), signal("qT_rounded", 2), signal("qT_ready", 2)
        tk_filled, kT_rounded, kT_ready = signal("tk_filled", 2), signal("kT_rounded", 2), signal("kT_ready", 2)
        tr_filled, qr_ready, krT_ready = signal("tr_filled", 2), signal("qr_ready", 2), signal("krT_ready", 1)
        sd_filled, top_ready, probs_ready = signal("sd_filled", 4), signal("top_ready", 4), signal("probs_ready", 8)
        inv_ready = signal("inv_ready", 1)
        pt_filled, probsT_ready, pv_done = signal("pt_filled", 4), signal("probsT_ready", 4), signal("pv_done", 4)
        yD_ready, yD_filled = signal("yD_ready", 8), signal("yD_filled", 2)
        yTD_rounded, yTD_ready = signal("yTD_rounded", 4), signal("yTD_ready", 4)
        u_ready, cp_filled, pooled_ready = signal("u_ready", MT), signal("cp_filled", 2), signal("pooled_ready", 2)
        cm_filled, yC_ready, yC_filled = signal("cm_filled", 2, primed=1), signal("yC_ready", 2), signal("yC_filled", 2)
        yTC_rounded, yTC_ready = signal("yTC_rounded", 4), signal("yTC_ready", 4)
        zb_ready, v_b_ready = signal("zb_ready", MT), signal("v_b_ready", MT)
        la_filled, soft_ready, la_ready = signal("la_filled", 2), signal("soft_ready", 2), signal("la_ready", 2, primed=1)
        cum_filled, e_ready = signal("cum_filled", 2), signal("e_ready", 4)
        rem_filled, e_rem_ready = signal("rem_filled", 2), signal("e_rem_ready", 2)
        tb_filled, q_b_ready, k_b_ready = signal("tb_filled", 2), signal("q_b_ready", 4), signal("k_b_ready", 2)
        k_dec_ready = signal("k_dec_ready", 4)
        sb_filled, picked_ready, score_b_ready = signal("sb_filled", 4), signal("picked_ready", 4), signal("score_b_ready", 2, primed=1)
        kv_filled, kv_kept, state_ready = signal("kv_filled", 6), signal("kv_kept", 12), signal("state_ready", 8)
        ob_filled, ob_squared, ob_ms_ready, ob_rs_ready = (
            signal("ob_filled", 2), signal("ob_squared", 2), signal("ob_ms_ready", 1), signal("ob_rs_ready", 1))
        yB_ready, yB_filled = signal("yB_ready", 8), signal("yB_filled", 2)
        yTB_rounded, yTB_ready = signal("yTB_rounded", 4), signal("yTB_ready", 4)
        z_rq_ready, z_rk_ready, v_a_ready = signal("z_rq_ready", MT), signal("z_rk_ready", MT), signal("v_a_ready", MT)
        rq_turned, rk_turned = signal("rq_turned", 2), signal("rk_turned", 2)
        aq_filled, qT_a_ready = signal("aq_filled", 2), signal("qT_a_ready", 2)
        ak_filled, kT_a_ready = signal("ak_filled", 2), signal("kT_a_ready", 2)
        sa_filled, score_a_ready = signal("sa_filled", 4), signal("score_a_ready", 4)
        oa_filled, oa_squared, oa_ms_ready, oa_rs_ready = (
            signal("oa_filled", 2), signal("oa_squared", 2), signal("oa_ms_ready", 1), signal("oa_rs_ready", 1))
        yA_ready, yA_filled = signal("yA_ready", 8, primed=1), signal("yA_filled", 2)
        yTA_rounded, yTA_ready = signal("yTA_rounded", 4, primed=1), signal("yTA_ready", 4, primed=1)

        def bcast(ap, axis, n):
            shape = list(ap.shape)
            assert shape[axis] == 1
            shape[axis] = n
            return ap.broadcast_to(shape)

        def per_head(s):
            return s.rearrange("p (m h o) -> p m h o", m=MT, o=1)

        block = ctx.enter_context(nc.Block())

        @block.sync
        def _(sp):
            with sp.Fori(0, DEPTH) as l:
                sp.wait_ge(*cm_filled.at(l, 0))
                sp.wait_ge(*la_ready.at(l, 0))
                sp.dma_start(mats[:], mats_in[l]).then_inc(mats_loaded.sem, 16)
                with sp.Fori(0, PER_RING) as k:
                    for r in range(RING):
                        sp.wait_ge(*split[r].at(l, k))
                        sp.dma_start(raw[r][:], stream[l, k, r]).then_inc(loaded[r].sem, 16)
            for c in range(4):
                sp.wait_ge(*added[c].at(DEPTH, 0))
                sp.dma_start(out.rearrange("(m p) (c n) -> c p m n", p=P, c=4)[c],
                             x[:, :, c * 512:(c + 1) * 512]).then_inc(stored.sem, 16)
            sp.wait_ge(stored.sem, 64)

        @block.tensor
        def _(pe):
            for sig in (*multiplied, cm_filled):
                pe.sem_inc(sig.sem, 1)
            pe.wait_ge(ident_loaded.sem, 16)
            ident = const("ident")

            with pe.Fori(0, DEPTH) as l:
                pos = [0]

                def granules(upto):
                    for j in range(pos[0], upto):
                        s, slots = PLAN[j]
                        name, width, src, base, n_slots, per = STAGES[s]
                        a, r = s % 2, j % RING
                        first = slots[0] == base
                        if first:
                            pe.wait_ge(*taken[a].at(l, MT * (s // 2)))
                        if name == "mq":
                            pe.wait_ge(*xT_ready.at(l, slots[-1] + 1))
                        if name == "wq0" and first:
                            pe.wait_ge(*lqT_ready.at(l, 4))
                        if name == "wkv0" and first:
                            pe.wait_ge(*lkT_ready.at(l, 2))
                        if name == "out0" and slots[0] % GT == 0:
                            pe.wait_ge(*(yTD_ready, yTC_ready, yTB_ready, yTA_ready)[slots[0] // GT].at(l, 4))
                        pe.wait_ge(*split[r].at(l, j // RING + 1))
                        t_hi, t_lo = (xT_hi, xT_lo) if src == "x" else (yT_hi, yT_lo)
                        for i, slot in enumerate(slots):
                            w_hi = hi[r][:, i * 512:i * 512 + width]
                            w_lo = lo[r][:, i * 512:i * 512 + width]
                            for m in range(MT):
                                a_hi = t_hi[:, slot, m * P:(m + 1) * P]
                                a_lo = t_lo[:, slot, m * P:(m + 1) * P]
                                acc = pair[a][m][:, 0:width]
                                last = slot == base + n_slots - 1
                                nc.tensor.matmul(acc, a_hi, w_hi, start=(slot == base), stop=False)
                                nc.tensor.matmul(acc, a_hi, w_lo, start=False, stop=False)
                                mm = nc.tensor.matmul(acc, a_lo, w_hi, start=False, stop=last)
                        mm.then_inc(multiplied[r].sem, 1)
                    pos[0] = upto

                def turn(b, tiles):
                    for i, tile in enumerate(tiles):
                        t = nc.tensor.transpose(bank[b][:, i * P:(i + 1) * P], tile, ident)
                    return t

                def turn_x(f):
                    turn(f % 4, [x[:, m, kt * P:(kt + 1) * P] for kt in (2 * f, 2 * f + 1)
                                 for m in range(MT)]).then_inc(x_filled.sem, 1)

                for f in range(8):
                    if f == 0:
                        pe.wait_ge(*yA_ready.at(l, 0))
                    if f == 2:
                        pe.wait_ge(*yTA_ready.at(l, 0))
                    if f >= 4:
                        pe.wait_ge(*xT_ready.at(l, 2 * (f - 4) + 2))
                    if f % 2 == 0:
                        pe.wait_ge(x_loaded[f // 2].sem, 16)
                        pe.wait_ge(*added[f // 2].at(l, 0))
                    turn_x(f)
                    if f == 5:
                        granules(1)
                    if f == 6:
                        granules(2)
                granules(11)

                for f in range(2):
                    pe.wait_ge(*zq_ready.at(l, MT))
                    pe.wait_ge(*xT_ready.at(l, 10 + 2 * f))
                    turn(f, [zq[:, m, kt * P:(kt + 1) * P] for kt in (2 * f, 2 * f + 1)
                             for m in range(MT)]).then_inc(lq_filled.sem, 1)
                granules(19)
                pe.wait_ge(*zlat_ready.at(l, MT))
                pe.wait_ge(*xT_ready.at(l, KT))
                turn(2, [zlat[:, m, kt * P:(kt + 1) * P] for kt in range(2)
                         for m in range(MT)]).then_inc(lk_filled.sem, 1)
                turn(3, [zlat[:, m, KV_RANK - WA_ROW:KV_RANK - WA_ROW + P]
                         for m in range(MT)]).then_inc(aT_filled.sem, 1)
                granules(38)

                for f in range(2):
                    pe.wait_ge(*lqT_ready.at(l, 2 * f + 2))
                    pe.wait_ge(*q_scaled.at(l, 1))
                    turn(f, [q_sb[:, m, h, 0:NOPE] for h in (2 * f, 2 * f + 1)
                             for m in range(MT)]).then_inc(tq_filled.sem, 1)
                granules(39)
                for f in range(2):
                    pe.wait_ge(*(lkT_ready, aT_ready)[f].at(l, (2, 1)[f]))
                    pe.wait_ge(*k_scaled.at(l, 1))
                    turn(2 + f, [kv_sb[:, m, h, 0:NOPE] for h in (2 * f, 2 * f + 1)
                                 for m in range(MT)]).then_inc(tk_filled.sem, 1)
                granules(42)
                pe.wait_ge(*q_turned.at(l, 1))
                pe.wait_ge(*qT_ready.at(l, 1))
                turn(0, [qr[:, m, 2 * a:2 * a + 2, :].rearrange("p h c -> p (h c)") for a in range(2)
                         for m in range(MT)]).then_inc(tr_filled.sem, 1)
                pe.wait_ge(*k_turned.at(l, 1))
                pe.wait_ge(*qT_ready.at(l, 2))
                turn(1, [kr[:, m, 2 * a:2 * a + 2, :].rearrange("p h c -> p (h c)") for a in range(2)
                         for m in range(MT)]).then_inc(tr_filled.sem, 1)
                granules(45)

                def scores_d(m):
                    for f in range(2):
                        b = (2 + 2 * m + f) % 4
                        if m == 0:
                            pe.wait_ge(*kT_ready.at(l, f + 1))
                        else:
                            pe.wait_ge(*(qr_ready, krT_ready)[f].at(l, (2, 1)[f]))
                        if m == 0 and f == 0:
                            pe.wait_ge(*qT_ready.at(l, 2))
                            pe.wait_ge(*kT_ready.at(l, 2))
                            pe.wait_ge(*qr_ready.at(l, 2))
                            pe.wait_ge(*krT_ready.at(l, 1))
                        for i, h in enumerate((2 * f, 2 * f + 1)):
                            acc = bank[b][:, i * SEQ:(i + 1) * SEQ]
                            q_hi = yT_hi[:, SLOT["B"] + h, m * P:(m + 1) * P]
                            q_lo = yT_lo[:, SLOT["B"] + h, m * P:(m + 1) * P]
                            k_hi, k_lo = yT_hi[:, SLOT["A"] + h, :], yT_lo[:, SLOT["A"] + h, :]
                            nc.tensor.matmul(acc, q_hi, k_hi, start=True, stop=False)
                            nc.tensor.matmul(acc, q_hi, k_lo, start=False, stop=False)
                            nc.tensor.matmul(acc, q_lo, k_hi, start=False, stop=False)
                            mm = nc.tensor.matmul(acc, q_heads[:, 0, f, i, m * P:(m + 1) * P], krT[:, f, :],
                                                  start=False, stop=True)
                        mm.then_inc(sd_filled.sem, 1)

                scores_d(0)
                granules(46)
                scores_d(1)
                granules(50)

                def turn_probs(h):
                    b = 2 + h % 2
                    if h < 2:
                        pe.wait_ge(*probs_ready.at(l, 8))
                    else:
                        pe.wait_ge(*probsT_ready.at(l, h - 1))
                    turn(b, [probs[:, m, h, j * P:(j + 1) * P] for j in range(MT)
                             for m in range(MT)]).then_inc(pt_filled.sem, 1)

                def times_v(h):
                    pe.wait_ge(*probsT_ready.at(l, h + 1))
                    for m in range(MT):
                        for j in range(MT):
                            mm = nc.tensor.matmul(bank[m][:, h * HD:(h + 1) * HD],
                                                  probsT[:, h % 2, j, m * P:(m + 1) * P],
                                                  kv_sb[:, j, h, NOPE:NOPE + HD],
                                                  start=(h == 0 and j == 0), stop=(h == 3 and j == 1),
                                                  skip_group_check=True)
                    mm.then_inc(pv_done.sem, 1)

                turn_probs(0)
                turn_probs(1)
                granules(51)
                times_v(0)
                times_v(1)
                turn_probs(2)
                turn_probs(3)
                granules(53)
                times_v(2)
                times_v(3)
                granules(57)

                def turn_y(b0, y, filled):
                    for f in range(2):
                        turn(b0 + f, [y[:, m, kt * P:(kt + 1) * P] for kt in (2 * f, 2 * f + 1)
                                      for m in range(MT)]).then_inc(filled.sem, 1)

                pe.wait_ge(*yD_ready.at(l, 8))
                pe.wait_ge(*probsT_ready.at(l, 4))
                turn_y(2, gate0, yD_filled)

                pe.wait_ge(*u_ready.at(l, MT))
                pe.wait_ge(consts_loaded.sem, 16)
                band = const("band").rearrange("p (g s t) -> p g s t", g=4, s=MT)
                for f in range(2):
                    for i, g in enumerate((2 * f, 2 * f + 1)):
                        acc = bank[f][:, i * SEQ:(i + 1) * SEQ]
                        nc.tensor.matmul(acc[:, 0:POOL_REACH], u[:, 0, g * P:(g + 1) * P], band[:, g, 0, :],
                                         start=True, stop=False, skip_group_check=True)
                        mm = nc.tensor.matmul(acc[:, SEQ - POOL_REACH:SEQ], u[:, 1, g * P:(g + 1) * P],
                                              band[:, g, 1, :], start=False, stop=True,
                                              skip_group_check=True)
                    mm.then_inc(cp_filled.sem, 1)
                granules(60)
                pe.wait_ge(*pooled_ready.at(l, 2))
                pe.wait_ge(*yTD_ready.at(l, 4))
                pe.wait_ge(*mats_loaded.at(l, 16))
                for m in range(MT):
                    for g in range(4):
                        mm = nc.tensor.matmul(bank[2 + m][:, g * P:(g + 1) * P],
                                              pooledT[:, g, m * P:(m + 1) * P],
                                              mats[:, M_POOL + g * P:M_POOL + (g + 1) * P],
                                              start=True, stop=True)
                    mm.then_inc(cm_filled.sem, 1)
                granules(63)
                pe.wait_ge(*yC_ready.at(l, 2))
                turn_y(0, gate1, yC_filled)

                pe.wait_ge(*aT_ready.at(l, 1))
                for m in range(MT):
                    nc.tensor.matmul(bank[2 + m][:], aT[:, m, :], mats[:, M_WA:M_WA + GROUP_W],
                                     start=True, stop=True).then_inc(la_filled.sem, 1)
                granules(68)
                pe.wait_ge(*la_ready.at(l, 2))
                pe.wait_ge(*yTC_ready.at(l, 4))
                for d, tri in enumerate(("tri_f", "tri_b")):
                    for f in range(2):
                        for m in range(MT):
                            at = d * 2 * P + f * P
                            mm = nc.tensor.matmul(bank[d][:, f * SEQ + m * P:f * SEQ + (m + 1) * P],
                                                  la[:, m, at:at + P], const(tri), start=True, stop=True)
                    mm.then_inc(cum_filled.sem, 1)
                for m in range(MT):
                    nc.tensor.matmul(bank[2 + m][:, 0:2 * P], const("after"), la[:, m, 0:2 * P],
                                     start=True, stop=True)
                    nc.tensor.matmul(bank[2 + m][:, 2 * P:4 * P], const("before"), la[:, m, 2 * P:4 * P],
                                     start=True, stop=True).then_inc(rem_filled.sem, 1)
                granules(71)
                pe.wait_ge(*zb_ready.at(l, MT))
                for a in range(2):
                    pe.wait_ge(*e_ready.at(l, 2 * a + 2))
                    turn(a, [zb[:, m, a, f * P:(f + 1) * P] for f in range(2)
                             for m in range(MT)]).then_inc(tb_filled.sem, 1)
                granules(74)

                def scores_b(m):
                    for d in range(2):
                        if m == 0:
                            pe.wait_ge(*e_rem_ready.at(l, d + 1))
                        for f in range(2):
                            mm = nc.tensor.matmul(
                                bank[(2 + 2 * m + d) % 4][:, f * SEQ:(f + 1) * SEQ],
                                e_neg[:, d, f, m * P:(m + 1) * P],
                                q_heads[:, d, f, :, m * P:(m + 1) * P], start=True, stop=True)
                        mm.then_inc(sb_filled.sem, 1)

                pe.wait_ge(*q_b_ready.at(l, 4))
                pe.wait_ge(*k_b_ready.at(l, 2))
                scores_b(0)
                scores_b(1)
                granules(76)

                def outer_kv(n, b, m, c, d):
                    for a in range(2):
                        mm = nc.tensor.matmul(bank[b][:, a * SEQ:(a + 1) * SEQ],
                                              k_dec[:, c, d, a * P:(a + 1) * P],
                                              v_b[:, m, a * SEQ:(a + 1) * SEQ], start=True, stop=True)
                    mm.then_inc(kv_filled.sem, 1)

                pe.wait_ge(*v_b_ready.at(l, MT))
                pe.wait_ge(*k_dec_ready.at(l, 2))
                pe.wait_ge(*picked_ready.at(l, 3))
                outer_kv(0, 2, 0, 0, 0)
                outer_kv(1, 3, 0, 1, 0)
                outer_kv(2, 0, 0, 1, 1)
                granules(78)
                pe.wait_ge(*k_dec_ready.at(l, 4))
                pe.wait_ge(*picked_ready.at(l, 4))
                outer_kv(3, 1, 1, 0, 0)
                pe.wait_ge(*kv_kept.at(l, 4))
                outer_kv(4, 2, 1, 1, 1)
                outer_kv(5, 3, 1, 0, 1)
                granules(82)
                pe.wait_ge(*score_b_ready.at(l, 2))
                pe.wait_ge(*state_ready.at(l, 8))
                pe.wait_ge(*kv_kept.at(l, 12))
                for m in range(MT):
                    for h in range(HEADS):
                        nc.tensor.matmul(bank[m][:, h * HD:(h + 1) * HD], score_b[:, m, h, :],
                                         v_b[:, m, h * HD:(h + 1) * HD], start=(h == 0), stop=False,
                                         skip_group_check=True)
                    for c in range(2):
                        n = 2 * m + c
                        for h in range(HEADS):
                            for d in range(2):
                                t = n - 1 if d == 0 else 2 - n
                                if t < 0:
                                    continue
                                mm = nc.tensor.matmul(
                                    bank[m][c * 64:(c + 1) * 64, h * HD:(h + 1) * HD],
                                    q_heads[:, d, h // 2, h % 2, n * GLA_CHUNK:(n + 1) * GLA_CHUNK],
                                    state[:, d, t, h // 2, :], start=False, stop=True,
                                    skip_group_check=True)
                    mm.then_inc(ob_filled.sem, 1)
                granules(88)
                pe.wait_ge(*yB_ready.at(l, 8))
                turn_y(2, gate0, yB_filled)
                granules(89)

                pe.wait_ge(*rq_turned.at(l, 2))
                for f in range(2):
                    turn(f, [rq_rot[:, m * HEADS + h, :] for h in (2 * f, 2 * f + 1)
                             for m in range(MT)]).then_inc(aq_filled.sem, 1)
                granules(94)
                pe.wait_ge(*rk_turned.at(l, 2))
                pe.wait_ge(*yTB_ready.at(l, 4))
                for f in range(2):
                    turn(2 + f, [rk_rot[:, m * HEADS + h, :] for h in (2 * f, 2 * f + 1)
                                 for m in range(MT)]).then_inc(ak_filled.sem, 1)
                granules(97)
                for h in range(HEADS):
                    if h % 2 == 0:
                        pe.wait_ge(*qT_a_ready.at(l, h // 2 + 1))
                        pe.wait_ge(*kT_a_ready.at(l, h // 2 + 1))
                    if h == 1:
                        pe.wait_ge(*qT_a_ready.at(l, 2))
                    if h == 2:
                        pe.wait_ge(*kT_a_ready.at(l, 2))
                    for j in range(MT):
                        mm = nc.tensor.matmul(bank[h][:, j * SEQ:(j + 1) * SEQ],
                                              kT_a[:, h, j * P:(j + 1) * P], qT_a[:, h, :],
                                              start=True, stop=True)
                    mm.then_inc(sa_filled.sem, 1)
                granules(100)
                pe.wait_ge(*v_a_ready.at(l, MT))
                pe.wait_ge(*score_a_ready.at(l, 4))
                for m in range(MT):
                    for h in range(HEADS):
                        for j in range(MT):
                            mm = nc.tensor.matmul(bank[m][:, h * HD:(h + 1) * HD],
                                                  score_a[:, h, j, m * P:(m + 1) * P],
                                                  v_a[:, j, h * HD:(h + 1) * HD],
                                                  start=(h == 0 and j == 0), stop=(h == 3 and j == 1),
                                                  skip_group_check=True)
                    mm.then_inc(oa_filled.sem, 1)
                granules(109)
                pe.wait_ge(*yA_ready.at(l, 8))
                turn_y(2, gate1, yA_filled)
                granules(GRANULES)

        @block.scalar
        def _(act):
            act.dma_start(const("ident"), consts_in[:, 0:P]).then_inc(ident_loaded.sem, 16)
            act.dma_start(gains_all[:], gains_in).then_inc(gains_loaded.sem, 16)
            for c in range(4):
                act.dma_start(x[:, :, c * 512:(c + 1) * 512],
                              x_in.rearrange("(m p) (c n) -> c p m n", p=P, c=4)[c]).then_inc(x_loaded[c].sem, 16)
            act.dma_start(consts[:, P:], consts_in[:, P:]).then_inc(consts_loaded.sem, 16)

            for sig in (*taken, yTA_rounded):
                act.sem_inc(sig.sem, 1)

            def square_x(c):
                for m in range(MT):
                    nc.scalar.activation(bank_free_scratch(m), x[:, m, c * 512:(c + 1) * 512], ACT.Square,
                                         accum_out=x_sq[:, m, c:c + 1]).then_inc(x_squared.sem, 1)

            def bank_free_scratch(m):
                return gate0[:, m, :]

            for c in range(3):
                act.wait_ge(x_loaded[c].sem, 16)
                if c > 0:
                    act.wait_ge(x_squared.sem, 2 * c)
                square_x(c)

            with act.Fori(0, DEPTH) as l:
                pos, step = [0], [0]

                def splits(upto):
                    for j in range(pos[0], upto):
                        r = j % RING
                        act.wait_ge(*loaded[r].at(l, 16 * (j // RING + 1)))
                        act.wait_ge(*multiplied[r].at(l, j // RING))
                        per, width = len(PLAN[j][1]), STAGES[PLAN[j][0]][1]
                        cut = [t[r][:].rearrange("p (i n) -> p i n", i=2)[:, 0:per, 0:width] for t in (hi, raw)]
                        nc.scalar.activation(cut[0], cut[1], ACT.Copy).then_inc(rounded[r].sem, 1)
                    pos[0] = upto

                def chained(ins):
                    step[0] += 1
                    ins.then_inc(act_step.sem, 1)
                    act.wait_ge(*act_step.at(l, step[0]))

                def stage_done(name):
                    act.wait_ge(*multiplied[(END[name] - 1) % RING].at(l, (END[name] - 1) // RING + 1))

                def take(name, dst, rs, ready, func=ACT.Copy, cols=512):
                    stage_done(name)
                    a = STAGE_OF[name] % 2
                    for m in range(MT):
                        nc.scalar.activation(dst(m), pair[a][m][:, 0:cols], func,
                                             scale=rs[:, m:m + 1]).then_inc(ready.sem, 1)
                    act.wait_ge(*ready.at(l, take_n[name]))
                    for m in range(MT):
                        act.sem_inc(taken[a].sem, 1)

                take_n = {"mq": 2, "lat": 2, "mg": 2, "wq0": 2, "wq1": 4, "wkv0": 2, "wkv1": 4, "pv": 2,
                          "pg": 2, "gqk": 2, "gv": 2, "gg": 4, "rq": 2, "rk": 2, "rv": 2, "rg": 4}

                def round_tiles(f0, filled, rounded_, dst, b0, gain, n_banks=2, slot0=0):
                    for f in range(n_banks):
                        act.wait_ge(*filled.at(l, f0 + f + 1))
                        for i in range(2):
                            kt = 2 * f + i
                            nc.scalar.activation(dst[:, slot0 + kt, :], bank[(b0 + f) % 4][:, i * SEQ:(i + 1) * SEQ],
                                                 ACT.Copy, scale=gains[:, gain + kt:gain + kt + 1]
                                                 ).then_inc(rounded_.sem, 1)

                splits(4)
                act.wait_ge(*gains_ready.at(l, 1))
                for f in range(0, 8, 2):
                    round_tiles(f, x_filled, xT_rounded, xT_hi, f % 4, G_NORM + 2 * f, slot0=2 * f)
                splits(6)
                act.wait_ge(*added[3].at(l, 0))
                act.wait_ge(x_loaded[3].sem, 16)
                act.wait_ge(*x_squared.at(l, 6))
                square_x(3)
                splits(10)
                act.wait_ge(*x_rs_ready.at(l, 1))
                take("mq", lambda m: zq[:, m, :], x_rs, zq_ready)
                for m in range(MT):
                    nc.scalar.activation(gate0[:, m, :], zq[:, m, :], ACT.Square,
                                         accum_out=lq_sq[:, m:m + 1]).then_inc(lq_squared.sem, 1)
                splits(13)
                round_tiles(0, lq_filled, lqT_rounded, yT_hi, 0, G_QN, slot0=SLOT["B"])
                splits(18)
                take("lat", lambda m: zlat[:, m, :], x_rs, zlat_ready, cols=LAT_W)
                act.wait_ge(*lq_squared.at(l, MT))
                for m in range(MT):
                    nc.scalar.activation(gate0[:, m, 0:KV_RANK], zlat[:, m, 0:KV_RANK], ACT.Square,
                                         accum_out=lk_sq[:, m:m + 1]).then_inc(lk_squared.sem, 1)
                    nc.scalar.activation(gate0[:, m, 256:256 + ROPE], zlat[:, m, LAT_W - ROPE:LAT_W], ACT.Square,
                                         accum_out=kpe_sq[:, m:m + 1]).then_inc(lk_squared.sem, 1)
                splits(21)
                round_tiles(0, lk_filled, lkT_rounded, yT_hi, 2, G_KVN, n_banks=1, slot0=SLOT["A"])
                act.wait_ge(*aT_filled.at(l, 1))
                if True:
                    act.wait_ge(cleared.sem, 5)
                nc.scalar.activation(aT[32:64, :, :], bank[3][32:64, 0:MT * P].rearrange("p (m t) -> p m t", m=MT),
                                     ACT.Copy).then_inc(aT_ready.sem, 1)
                splits(26)
                act.wait_ge(*lk_squared.at(l, 2 * MT))
                take("mg", lambda m: gate0[:, m, :], x_rs, gate0_ready, func=ACT.Silu)
                splits(28)
                act.wait_ge(*lq_rs_ready.at(l, 1))
                take("wq0", lambda m: q_sb[:, m, 0:2, :].rearrange("p h c -> p (h c)"), lq_rs, q_ready, cols=2 * QK_W)
                splits(30)
                take("wq1", lambda m: q_sb[:, m, 2:4, :].rearrange("p h c -> p (h c)"), lq_rs, q_ready, cols=2 * QK_W)
                act.wait_ge(*q_ready.at(l, 4))
                for m in range(MT):
                    if m:
                        act.wait_ge(*q_sq_read.at(l, m))
                    nc.scalar.activation(sq_d, q_sb[:, m].rearrange("p h c -> p (h c)"), ACT.Square
                                         ).then_inc(q_squared.sem, 1)
                    if m == 0:
                        splits(32)
                        act.wait_ge(*lk_rs_ready.at(l, 1))
                        take("wkv0", lambda m: kv_sb[:, m, 0:2, :].rearrange("p h c -> p (h c)"), lk_rs, kv_ready)
                splits(34)
                take("wkv1", lambda m: kv_sb[:, m, 2:4, :].rearrange("p h c -> p (h c)"), lk_rs, kv_ready)
                for m in range(MT):
                    act.wait_ge(*q_sq_read.at(l, 2 + m))
                    nc.scalar.activation(sq_d[:, 0:512].rearrange("p (h c) -> p h c", h=HEADS),
                                         kv_sb[:, m, :, 0:NOPE], ACT.Square).then_inc(k_squared.sem, 1)
                    splits(35 + m)
                splits(40)
                for f in range(2):
                    act.wait_ge(*tq_filled.at(l, f + 1))
                    nc.scalar.activation(yT_hi[:, SLOT["B"] + 2 * f:SLOT["B"] + 2 * f + 2, :].rearrange("p h t -> p (h t)"),
                                         bank[f][:], ACT.Copy, scale=gains[:, G_QK:G_QK + 1]
                                         ).then_inc(qT_rounded.sem, 1)
                splits(41)
                for f in range(2):
                    act.wait_ge(*tk_filled.at(l, f + 1))
                    nc.scalar.activation(yT_hi[:, SLOT["A"] + 2 * f:SLOT["A"] + 2 * f + 2, :].rearrange("p h t -> p (h t)"),
                                         bank[2 + f][:], ACT.Copy, scale=gains[:, G_QK + 1:G_QK + 2]
                                         ).then_inc(kT_rounded.sem, 1)
                splits(42)
                take("pv", lambda m: u[:, m, :], x_rs, u_ready)
                splits(44)
                act.wait_ge(*tr_filled.at(l, 1))
                act.wait_ge(cleared.sem, 5)
                for i in range(2):
                    nc.scalar.activation(q_heads[64 * i:64 * i + 64, 0, :, i, :],
                                         bank[0][64 * i:64 * i + 64, :].rearrange("p (a t) -> p a t", a=2),
                                         ACT.Copy).then_inc(qr_ready.sem, 1)
                act.wait_ge(*tr_filled.at(l, 2))
                nc.scalar.activation(krT[:].rearrange("p a t -> p (a t)"), bank[1][:], ACT.Copy
                                     ).then_inc(krT_ready.sem, 1)
                for m in range(MT):
                    splits(47 + m)
                    for f in range(2):
                        n = 2 * m + f
                        act.wait_ge(*top_ready.at(l, n + 1))
                        for i in range(2):
                            h = 2 * f + i
                            at = m * HEADS + h
                            nc.scalar.activation(probs[:, m, h, :], bank[(2 + n) % 4][:, i * SEQ:(i + 1) * SEQ],
                                                 ACT.Exp, bias=neg_top[:, at:at + 1], scale=QK_W ** -0.5,
                                                 accum_out=p_sum[:, at:at + 1]).then_inc(probs_ready.sem, 1)
                splits(50)
                take("pg", lambda m: gate1[:, m, :], x_rs, gate1_ready, func=ACT.Silu)
                splits(58)
                act.wait_ge(*pv_done.at(l, 4))
                take("gqk", lambda m: zb[:, m].rearrange("p a c -> p (a c)"), x_rs, zb_ready)
                splits(59)
                round_tiles(0, yD_filled, yTD_rounded, yT_hi, 2, G_Y + SLOT["D"], slot0=SLOT["D"])
                for f in range(2):
                    act.wait_ge(*cp_filled.at(l, f + 1))
                    nc.scalar.activation(pooledT[:, 2 * f:2 * f + 2, :].rearrange("p g t -> p (g t)"), bank[f][:],
                                         ACT.Copy).then_inc(pooled_ready.sem, 1)
                splits(65)
                round_tiles(0, yC_filled, yTC_rounded, yT_hi, 0, G_Y + SLOT["C"], slot0=SLOT["C"])
                for m in range(MT):
                    act.wait_ge(*la_filled.at(l, m + 1))
                    chained(nc.scalar.activation(la[:, m, :], bank[2 + m][:], ACT.Abs))
                for m in range(MT):
                    chained(nc.scalar.activation(la[:, m, :], la[:, m, :], ACT.Exp, scale=-1.0))
                for m in range(MT):
                    nc.scalar.activation(la[:, m, :], la[:, m, :], ACT.Ln, bias=1.0).then_inc(soft_ready.sem, 1)
                splits(66)
                take("gv", lambda m: v_b[:, m, :], x_rs, v_b_ready)
                splits(70)
                for d in range(2):
                    act.wait_ge(*cum_filled.at(l, d + 1))
                    for dst, sign in ((e_pos, 1.0), (e_neg, -1.0)):
                        nc.scalar.activation(dst[:, d].rearrange("p f t -> p (f t)"), bank[d][:], ACT.Exp,
                                             scale=sign / GLA_TAU).then_inc(e_ready.sem, 1)
                for m in range(MT):
                    act.wait_ge(*rem_filled.at(l, m + 1))
                    nc.scalar.activation(e_rem[:, m].rearrange("p d c -> p (d c)"), bank[2 + m][:], ACT.Exp,
                                         scale=1.0 / GLA_TAU).then_inc(e_rem_ready.sem, 1)
                splits(74)
                act.wait_ge(*yD_filled.at(l, 2))
                take("gg", lambda m: gate0[:, m, :], x_rs, gate0_ready, func=ACT.Silu)
                splits(78)

                def keep(n, b, d, t):
                    act.wait_ge(*kv_filled.at(l, n + 1))
                    for i in range(2):
                        nc.scalar.activation(
                            state[64 * i:64 * i + 64, d, t, :, :],
                            bank[b][64 * i:64 * i + 64, :].rearrange("p (a e) -> p a e", a=2)[:, :, i * HD:(i + 1) * HD],
                            ACT.Copy).then_inc(kv_kept.sem, 1)

                keep(0, 2, 0, 0)
                keep(1, 3, 0, 1)
                keep(2, 0, 1, 2)
                splits(80)
                keep(3, 1, 0, 2)
                keep(4, 2, 1, 0)
                keep(5, 3, 1, 1)
                splits(82)
                act.wait_ge(*yC_filled.at(l, 2))
                take("rq", lambda m: gate1[:, m, :], x_rs, z_rq_ready)
                splits(84)
                for m in range(MT):
                    act.wait_ge(*ob_filled.at(l, m + 1))
                    if m:
                        act.wait_ge(*ob_sq_read.at(l, m))
                    nc.scalar.activation(sq_b, bank[m][:], ACT.Square).then_inc(ob_squared.sem, 1)
                splits(90)
                round_tiles(0, yB_filled, yTB_rounded, yT_hi, 2, G_Y + SLOT["B"], slot0=SLOT["B"])
                take("rk", lambda m: z_rk[:, m, :], x_rs, z_rk_ready)
                splits(91)
                for f in range(2):
                    act.wait_ge(*aq_filled.at(l, f + 1))
                    nc.scalar.activation(qT_a[:, 2 * f:2 * f + 2, :].rearrange("p h t -> p (h t)"), bank[f][:],
                                         ACT.Copy).then_inc(qT_a_ready.sem, 1)
                splits(96)
                for f in range(2):
                    act.wait_ge(*ak_filled.at(l, f + 1))
                    nc.scalar.activation(kT_a[:, 2 * f:2 * f + 2, :].rearrange("p h t -> p (h t)"), bank[2 + f][:],
                                         ACT.Copy).then_inc(kT_a_ready.sem, 1)
                splits(98)
                take("rv", lambda m: v_a[:, m, :], x_rs, v_a_ready)
                splits(102)
                for m in range(MT):
                    act.wait_ge(*oa_filled.at(l, m + 1))
                    if m:
                        act.wait_ge(*oa_sq_read.at(l, m))
                    nc.scalar.activation(sq_a, bank[m][:], ACT.Square).then_inc(oa_squared.sem, 1)
                splits(106)
                take("rg", lambda m: gate1[:, m, :], x_rs, gate1_ready, func=ACT.Silu)
                splits(111)
                round_tiles(0, yA_filled, yTA_rounded, yT_hi, 2, G_Y + SLOT["A"], slot0=SLOT["A"])
                for c in range(3):
                    splits(114 + 8 * c)
                    act.wait_ge(*added[c].at(l, MT))
                    act.wait_ge(*x_squared.at(l, 8 + 2 * c))
                    square_x(c)
                splits(GRANULES)
                assert step[0] == act_step.per_layer, step[0]

        @block.vector
        def _(dve):
            for sig in (*split, *added, yA_ready, yTA_ready, la_ready, score_b_ready):
                dve.sem_inc(sig.sem, 1)
            with dve.Fori(0, DEPTH) as l:
                pos, step = [0], [0]

                def splits(upto):
                    for j in range(pos[0], upto):
                        r = j % RING
                        dve.wait_ge(*rounded[r].at(l, j // RING + 1))
                        per, width = len(PLAN[j][1]), STAGES[PLAN[j][0]][1]
                        cut = [t[r][:].rearrange("p (i n) -> p i n", i=2)[:, 0:per, 0:width] for t in (lo, raw, hi)]
                        nc.vector.tensor_tensor(cut[0], cut[1], cut[2].bitcast(F32), ALU.subtract
                                                ).then_inc(split[r].sem, 1)
                    pos[0] = upto

                def chained(ins):
                    step[0] += 1
                    ins.then_inc(dve_step.sem, 1)
                    dve.wait_ge(*dve_step.at(l, step[0]))

                def lo_tiles(rounded_, ready, dst_hi, dst_lo, b0, gain, n_banks=2, slot0=0, r0=0):
                    for f in range(n_banks):
                        dve.wait_ge(*rounded_.at(l, r0 + 2 * f + 2))
                        for i in range(2):
                            kt = 2 * f + i
                            nc.vector.scalar_tensor_tensor(
                                out=dst_lo[:, slot0 + kt, :], in0=bank[(b0 + f) % 4][:, i * SEQ:(i + 1) * SEQ],
                                scalar=gains[:, gain + kt:gain + kt + 1], in1=dst_hi[:, slot0 + kt, :].bitcast(F32),
                                op0=ALU.mult, op1=ALU.subtract).then_inc(ready.sem, 1)

                def mean_square(sq, ms, width, ready):
                    nc.vector.tensor_scalar(ms, sq, 1.0 / width, EPS, ALU.mult, ALU.add).then_inc(ready.sem, 1)

                dve.wait_ge(gains_loaded.sem, 16)
                dve.wait_ge(*yTA_rounded.at(l, 0))
                nc.vector.tensor_copy(gains[:], gains_all[:, bass.ds(l * GAIN_W, GAIN_W)]).then_inc(gains_ready.sem, 1)
                splits(4)
                dve.wait_ge(*gains_ready.at(l, 1))
                for f in range(0, 8, 2):
                    lo_tiles(xT_rounded, xT_ready, xT_hi, xT_lo, f % 4, G_NORM + 2 * f, slot0=2 * f, r0=2 * f)
                splits(8)
                dve.wait_ge(*x_squared.at(l, 8))
                chained(nc.vector.tensor_reduce(x_ms, x_sq, AX_X, ALU.add))
                mean_square(x_ms, x_ms, D_MODEL, x_ms_ready)
                splits(12)
                dve.wait_ge(*lq_squared.at(l, MT))
                mean_square(lq_sq, lq_ms, Q_RANK, lq_ms_ready)
                splits(13)
                lo_tiles(lqT_rounded, lqT_ready, yT_hi, yT_lo, 0, G_QN, slot0=SLOT["B"])
                dve.wait_ge(consts_loaded.sem, 16)
                dve.wait_ge(*score_b_ready.at(l, 0))
                for d, tri in enumerate(("tri_f", "tri_b")):
                    nc.vector.tensor_scalar(keep_bits[:, d, :], const(tri), -1.0, None, ALU.mult
                                            ).then_inc(bits_ready.sem, 1)
                splits(20)
                dve.wait_ge(*lk_squared.at(l, 2 * MT))
                mean_square(lk_sq, lk_ms, KV_RANK, lk_ms_ready)
                splits(21)
                lo_tiles(lkT_rounded, lkT_ready, yT_hi, yT_lo, 2, G_KVN, n_banks=1, slot0=SLOT["A"])
                splits(31)
                dve.wait_ge(*q_squared.at(l, 1))
                nc.vector.tensor_reduce(q_sq[:, 0:HEADS], sq_d.rearrange("p (h c) -> p h c", h=HEADS), AX_X,
                                        ALU.add).then_inc(q_sq_read.sem, 1)
                splits(33)
                dve.wait_ge(*q_squared.at(l, 2))
                nc.vector.tensor_reduce(q_sq[:, HEADS:], sq_d.rearrange("p (h c) -> p h c", h=HEADS), AX_X,
                                        ALU.add).then_inc(q_sq_read.sem, 1)
                dve.wait_ge(*q_sq_read.at(l, 2))
                mean_square(q_sq, q_ms, QK_W, q_ms_ready)
                for m in range(MT):
                    splits(35 + m)
                    dve.wait_ge(*k_squared.at(l, m + 1))
                    nc.vector.tensor_reduce(k_sq[:, m * HEADS:(m + 1) * HEADS],
                                            sq_d[:, 0:512].rearrange("p (h c) -> p h c", h=HEADS), AX_X,
                                            ALU.add).then_inc(q_sq_read.sem, 1)
                for m in range(MT):
                    dve.wait_ge(*q_sq_read.at(l, 4))
                    at = k_sq[:, m * HEADS:(m + 1) * HEADS]
                    chained(nc.vector.tensor_scalar(at, at, kpe_sq[:, m:m + 1], None, ALU.add))
                mean_square(k_sq, k_ms, QK_W, k_ms_ready)
                dve.wait_ge(*q_rs_ready.at(l, 1))
                nc.vector.tensor_tensor(q_sb[:], q_sb[:], bcast(per_head(q_rs), 3, QK_W), ALU.mult
                                        ).then_inc(q_scaled.sem, 1)
                dve.wait_ge(*k_rs_ready.at(l, 1))
                nc.vector.tensor_tensor(kv_sb[:, :, :, 0:NOPE], kv_sb[:, :, :, 0:NOPE], bcast(per_head(k_rs), 3, NOPE),
                                        ALU.mult).then_inc(k_scaled.sem, 1)
                splits(38)
                dve.wait_ge(*q_scaled.at(l, 1))
                dve.wait_ge(*tabs_ready.at(l, 6))
                half = ROPE // 2

                def table(which, part, n):
                    return bcast(rope_tab[:, which, part].rearrange("p m (o c) -> p m o c", o=1), 2, n)

                chained(nc.vector.tensor_tensor(qr[:], q_sb[:, :, :, NOPE:], table(0, 0, HEADS), ALU.mult))
                for a in range(2):
                    chained(nc.vector.tensor_tensor(
                        rot_d[:, :, :, a * half:(a + 1) * half],
                        q_sb[:, :, :, NOPE + (1 - a) * half:NOPE + (2 - a) * half],
                        table(0, 1, HEADS)[:, :, :, a * half:(a + 1) * half], ALU.mult))
                nc.vector.tensor_tensor(qr[:], qr[:], rot_d[:], ALU.add).then_inc(q_turned.sem, 1)
                zpe = zlat[:, :, LAT_W - ROPE:LAT_W]
                chained(nc.vector.tensor_tensor(kpe[:], zpe, rope_tab[:, 1, 0], ALU.mult))
                for a in range(2):
                    chained(nc.vector.tensor_tensor(kpe_x[:, :, a * half:(a + 1) * half],
                                                    zpe[:, :, (1 - a) * half:(2 - a) * half],
                                                    rope_tab[:, 1, 1, :, a * half:(a + 1) * half], ALU.mult))
                chained(nc.vector.tensor_tensor(kpe[:], kpe[:], kpe_x[:], ALU.add))
                nc.vector.tensor_tensor(kr[:], bcast(kpe[:].rearrange("p m (o c) -> p m o c", o=1), 2, HEADS),
                                        bcast(per_head(k_rs), 3, ROPE), ALU.mult).then_inc(k_turned.sem, 1)

                def lo_pair(rounded_, ready, b0, slot0, gain):
                    for f in range(2):
                        dve.wait_ge(*rounded_.at(l, f + 1))
                        at = slice(slot0 + 2 * f, slot0 + 2 * f + 2)
                        nc.vector.scalar_tensor_tensor(
                            out=yT_lo[:, at, :].rearrange("p h t -> p (h t)"), in0=bank[b0 + f][:],
                            scalar=gains[:, gain:gain + 1],
                            in1=yT_hi[:, at, :].rearrange("p h t -> p (h t)").bitcast(F32),
                            op0=ALU.mult, op1=ALU.subtract).then_inc(ready.sem, 1)

                splits(40)
                lo_pair(qT_rounded, qT_ready, 0, SLOT["B"], G_QK)
                splits(41)
                lo_pair(kT_rounded, kT_ready, 2, SLOT["A"], G_QK + 1)
                for m in range(MT):
                    splits(47 + m)
                    for f in range(2):
                        n = 2 * m + f
                        dve.wait_ge(*sd_filled.at(l, n + 1))
                        at = slice(2 * n, 2 * n + 2)
                        chained(nc.vector.tensor_reduce(top[:, at], bank[(2 + n) % 4][:].rearrange("p (h j) -> p h j", h=2),
                                                        AX_X, ALU.max))
                        nc.vector.tensor_scalar(neg_top[:, at], top[:, at], -QK_W ** -0.5, None, ALU.mult
                                                ).then_inc(top_ready.sem, 1)
                splits(51)
                dve.wait_ge(*probs_ready.at(l, 8))
                nc.vector.reciprocal(p_inv, p_sum).then_inc(inv_ready.sem, 1)

                def keep_probsT(h):
                    dve.wait_ge(*pt_filled.at(l, h + 1))
                    if h >= 2:
                        dve.wait_ge(*pv_done.at(l, h - 1))
                    nc.vector.tensor_copy(probsT[:, h % 2].rearrange("p j t -> p (j t)"), bank[2 + h % 2][:]
                                          ).then_inc(probsT_ready.sem, 1)

                keep_probsT(0)
                keep_probsT(1)
                splits(54)
                keep_probsT(2)
                keep_probsT(3)
                splits(56)
                dve.wait_ge(*pv_done.at(l, 4))
                dve.wait_ge(*gate0_ready.at(l, MT))
                dve.wait_ge(*inv_ready.at(l, 1))

                def gated(b, y, m, scales, ready):
                    for h in range(HEADS):
                        at = slice(h * HD, (h + 1) * HD)
                        nc.vector.scalar_tensor_tensor(
                            out=y[:, m, at], in0=bank[b][:, at], scalar=scales[:, m * HEADS + h:m * HEADS + h + 1],
                            in1=y[:, m, at], op0=ALU.mult, op1=ALU.mult).then_inc(ready.sem, 1)

                for m in range(MT):
                    gated(m, gate0, m, p_inv, yD_ready)
                splits(59)
                lo_tiles(yTD_rounded, yTD_ready, yT_hi, yT_lo, 2, G_Y + SLOT["D"], slot0=SLOT["D"])
                splits(62)
                dve.wait_ge(*gate1_ready.at(l, MT))
                for m in range(MT):
                    dve.wait_ge(*cm_filled.at(l, m + 1))
                    nc.vector.tensor_tensor(gate1[:, m, :], bank[2 + m][:], gate1[:, m, :], ALU.mult
                                            ).then_inc(yC_ready.sem, 1)
                splits(65)
                lo_tiles(yTC_rounded, yTC_ready, yT_hi, yT_lo, 0, G_Y + SLOT["C"], slot0=SLOT["C"])
                for m in range(MT):
                    dve.wait_ge(*soft_ready.at(l, m + 1))
                    nc.vector.scalar_tensor_tensor(out=la[:, m, :], in0=bank[2 + m][:], scalar=0.0, in1=la[:, m, :],
                                                   op0=ALU.min, op1=ALU.subtract).then_inc(la_ready.sem, 1)
                splits(72)
                dve.wait_ge(*tb_filled.at(l, 1))
                dve.wait_ge(*e_ready.at(l, 4))
                for d in range(2):
                    for i in range(2):
                        rows = slice(64 * i, 64 * i + 64)
                        nc.vector.scalar_tensor_tensor(
                            out=q_heads[rows, d, :, i, :], in0=bank[0][rows, :].rearrange("p (f t) -> p f t", f=2),
                            scalar=GLA_DK ** -0.5, in1=e_pos[rows, d], op0=ALU.mult, op1=ALU.mult
                            ).then_inc(q_b_ready.sem, 1)
                dve.wait_ge(*tb_filled.at(l, 2))
                for d in range(2):
                    nc.vector.tensor_tensor(e_neg[:, d].rearrange("p f t -> p (f t)"), bank[1][:],
                                            e_neg[:, d].rearrange("p f t -> p (f t)"), ALU.mult
                                            ).then_inc(k_b_ready.sem, 1)

                def decay_k(m):
                    for c in range(2):
                        rows = slice(64 * c, 64 * c + 64)
                        nc.vector.tensor_tensor(k_dec[rows, c], bcast(zb[rows, m, 1:2, :], 1, 2), e_rem[rows, m],
                                                ALU.mult).then_inc(k_dec_ready.sem, 1)

                splits(75)
                dve.wait_ge(*e_rem_ready.at(l, 2))
                dve.wait_ge(cleared.sem, 5)
                decay_k(0)

                dve.wait_ge(*bits_ready.at(l, 2))

                def pick(m):
                    for d, dst in enumerate((score_b[:, m], picked)):
                        dve.wait_ge(*sb_filled.at(l, 2 * m + d + 1))
                        if m == 1 and d == 1:
                            dve.wait_ge(*score_b_ready.at(l, 1))
                        nc.vector.tensor_tensor(
                            dst.bitcast(I32), bank[(2 + 2 * m + d) % 4][:].rearrange("p (h i) -> p h i", h=HEADS).bitcast(I32),
                            bcast(keep_bits[:, d:d + 1, :], 1, HEADS), ALU.bitwise_and).then_inc(picked_ready.sem, 1)
                    dve.wait_ge(*picked_ready.at(l, 2 * m + 2))
                    nc.vector.tensor_tensor(score_b[:, m], score_b[:, m], picked[:], ALU.add
                                            ).then_inc(score_b_ready.sem, 1)

                splits(76)
                pick(0)
                splits(77)
                pick(1)
                dve.wait_ge(*kv_filled.at(l, 3))
                decay_k(1)
                splits(82)
                dve.wait_ge(*kv_kept.at(l, 12))
                for t in (1, 2):
                    for d in range(2):
                        edge = GLA_CHUNK * (t + 1) - 1 if d == 0 else GLA_CHUNK * (3 - t)
                        for a in range(2):
                            if t == 2:
                                dve.wait_ge(*state_ready.at(l, 2 * d + a + 1))
                            nc.vector.scalar_tensor_tensor(
                                out=state[:, d, t, a, :], in0=state[:, d, t - 1, a, :],
                                scalar=e_pos[:, d, a, edge:edge + 1], in1=state[:, d, t, a, :],
                                op0=ALU.mult, op1=ALU.add).then_inc(state_ready.sem, 1)

                def head_squares(sq, m, squared, read):
                    dve.wait_ge(*squared.at(l, m + 1))
                    nc.vector.tensor_reduce(o_sq[:, m * HEADS:(m + 1) * HEADS], sq.rearrange("p (h c) -> p h c", h=HEADS),
                                            AX_X, ALU.add).then_inc(read.sem, 1)

                splits(84)
                for m in range(MT):
                    head_squares(sq_b, m, ob_squared, ob_sq_read)
                dve.wait_ge(*ob_sq_read.at(l, 2))
                mean_square(o_sq, o_ms, HD, ob_ms_ready)

                def turn_heads(z, z_ready, rot, turned):
                    hh = HD // 2
                    dve.wait_ge(*z_ready.at(l, MT))
                    zz = z[:].rearrange("p m (n c) -> p m n c", c=hh)
                    rr = rot[:].rearrange("p (m h) (a c) -> p m (h a) c", m=MT, a=2)

                    def tab(name, n):
                        return bcast(const(name).rearrange("p (m o c) -> p m o c", m=MT, o=1), 2, n)

                    chained(nc.vector.tensor_tensor(rr, zz, tab("rcos", 2 * HEADS), ALU.mult))
                    za = z[:].rearrange("p m (h a c) -> p m h a c", h=HEADS, a=2)
                    ta = rot_a[:].rearrange("p (m h) (a c) -> p m h a c", m=MT, a=2)
                    ra = rot[:].rearrange("p (m h) (a c) -> p (m h) a c", m=MT, a=2)
                    tb = rot_a[:].rearrange("p (m h) (a c) -> p (m h) a c", m=MT, a=2)
                    for a in range(2):
                        chained(nc.vector.tensor_tensor(ta[:, :, :, a, :], za[:, :, :, 1 - a, :], tab("rsin", HEADS),
                                                        ALU.mult))
                    for a, op in enumerate((ALU.subtract, ALU.add)):
                        nc.vector.tensor_tensor(ra[:, :, a, :], ra[:, :, a, :], tb[:, :, a, :], op
                                                ).then_inc(turned.sem, 1)

                splits(86)
                dve.wait_ge(*ob_rs_ready.at(l, 1))
                dve.wait_ge(*gate0_ready.at(l, 2 * MT))
                for m in range(MT):
                    gated(m, gate0, m, o_rs, yB_ready)
                turn_heads(gate1, z_rq_ready, rq_rot, rq_turned)
                splits(90)
                lo_tiles(yTB_rounded, yTB_ready, yT_hi, yT_lo, 2, G_Y + SLOT["B"], slot0=SLOT["B"])
                splits(91)
                dve.wait_ge(*rq_turned.at(l, 2))
                turn_heads(z_rk, z_rk_ready, rk_rot, rk_turned)
                splits(99)
                decay = const("decay").rearrange("p (h k i) -> p h k i", h=HEADS, k=3)
                for h in range(HEADS):
                    dve.wait_ge(*sa_filled.at(l, h + 1))
                    tiles = bank[h][:].rearrange("p (j i) -> p j i", j=4)
                    dst = score_a[:, h].rearrange("p j (m i) -> p (j m) i", m=MT)
                    chained(nc.vector.tensor_tensor(dst[:, 0:4:3], tiles[:, 0:4:3], bcast(decay[:, h, 0:1], 1, 2),
                                                    ALU.mult))
                    nc.vector.tensor_tensor(dst[:, 1:3], tiles[:, 1:3], decay[:, h, 1:3], ALU.mult
                                            ).then_inc(score_a_ready.sem, 1)
                splits(102)
                for m in range(MT):
                    head_squares(sq_a, m, oa_squared, oa_sq_read)
                dve.wait_ge(*oa_sq_read.at(l, 2))
                mean_square(o_sq, o_ms, HD, oa_ms_ready)
                splits(107)
                dve.wait_ge(*oa_rs_ready.at(l, 1))
                dve.wait_ge(*gate1_ready.at(l, 2 * MT))
                for m in range(MT):
                    gated(m, gate1, m, o_rs, yA_ready)
                splits(111)
                lo_tiles(yTA_rounded, yTA_ready, yT_hi, yT_lo, 2, G_Y + SLOT["A"], slot0=SLOT["A"])
                for c in range(4):
                    splits(min(114 + 8 * c, GRANULES))
                    j = END[f"out{c}"] - 1
                    dve.wait_ge(*multiplied[j % RING].at(l, j // RING + 1))
                    for m in range(MT):
                        at = x[:, m, c * 512:(c + 1) * 512]
                        nc.vector.tensor_tensor(at, pair[STAGE_OF[f"out{c}"] % 2][m][:], at, ALU.add
                                                ).then_inc(added[c].sem, 1)
                    dve.wait_ge(*added[c].at(l, MT))
                    for m in range(MT):
                        dve.sem_inc(taken[STAGE_OF[f"out{c}"] % 2].sem, 1)
                assert step[0] == dve_step.per_layer, step[0]

        @block.gpsimd
        def _(pool):
            pool.memset(minus_half, -0.5).then_inc(cleared.sem, 1)
            pool.memset(aT[:], 0.0).then_inc(cleared.sem, 1)
            pool.memset(q_heads[:], 0.0).then_inc(cleared.sem, 1)
            pool.memset(k_dec[:], 0.0).then_inc(cleared.sem, 1)
            pool.wait_ge(cleared.sem, 4)
            pool.memset(aT[64:65, :, :], 1.0).then_inc(cleared.sem, 1)

            with pool.Fori(0, DEPTH) as l:
                def rsqrt(ms, rs, ms_ready, rs_ready):
                    pool.wait_ge(*ms_ready.at(l, 1))
                    n = ms.shape[1]
                    pool.tensor_tensor(rs, ms, minus_half[:, 0:n], ALU.pow).then_inc(rs_ready.sem, 1)

                pool.wait_ge(cleared.sem, 5)
                pool.wait_ge(consts_loaded.sem, 16)
                rsqrt(x_ms, x_rs, x_ms_ready, x_rs_ready)
                pool.wait_ge(*mats_loaded.at(l, 16))
                half = ROPE // 2
                mcos, msin, mnsin = (const(n).rearrange("p (m c) -> p m c", m=MT) for n in ("mcos", "msin", "mnsin"))
                for w in range(2):
                    g = mats[:, M_ROPE + w * ROPE:M_ROPE + (w + 1) * ROPE]
                    g0 = bcast(g[:, 0:half].rearrange("p (o c) -> p o c", o=1), 1, MT)
                    g1 = bcast(g[:, half:].rearrange("p (o c) -> p o c", o=1), 1, MT)
                    gm = bcast(g.rearrange("p (o a c) -> p o a c", o=1, a=2), 1, MT)
                    cm = bcast(mcos.rearrange("p m (o c) -> p m o c", o=1), 2, 2)
                    pool.tensor_tensor(rope_tab[:, w, 0].rearrange("p m (a c) -> p m a c", a=2), gm, cm, ALU.mult
                                       ).then_inc(tabs_ready.sem, 1)
                    pool.tensor_tensor(rope_tab[:, w, 1, :, 0:half], g1, mnsin, ALU.mult).then_inc(tabs_ready.sem, 1)
                    pool.tensor_tensor(rope_tab[:, w, 1, :, half:], g0, msin, ALU.mult).then_inc(tabs_ready.sem, 1)
                rsqrt(lq_ms, lq_rs, lq_ms_ready, lq_rs_ready)
                rsqrt(lk_ms, lk_rs, lk_ms_ready, lk_rs_ready)
                rsqrt(q_ms, q_rs, q_ms_ready, q_rs_ready)
                rsqrt(k_ms, k_rs, k_ms_ready, k_rs_ready)
                rsqrt(o_ms, o_rs, ob_ms_ready, ob_rs_ready)
                rsqrt(o_ms, o_rs, oa_ms_ready, oa_rs_ready)


def shape_constants():
    import numpy as np

    c = np.zeros((P, CONST_W), np.float64)

    def put(name, value):
        at, w = CONSTS[name]
        c[:, at:at + w] = np.asarray(value, np.float64).reshape(P, w)

    i = np.arange(P)
    k, t = i[:, None], i[None, :]
    same = (k // GLA_CHUNK) == (t // GLA_CHUNK)
    put("ident", k == t)
    put("tri_f", same & (k <= t))
    put("tri_b", same & (k >= t))
    put("after", same & (k > t))
    put("before", same & (k < t))
    gamma = 1.0 - 2.0 ** (-5.0 - np.arange(HEADS))
    decay = np.zeros((P, HEADS, 3, P))
    for h in range(HEADS):
        f, b = gamma[h], gamma[HEADS - 1 - h]
        decay[:, h, 0] = np.where(t >= k, f ** (1.0 * np.abs(t - k)), 0) + np.where(k >= t, b ** (1.0 * np.abs(t - k)), 0)
        decay[:, h, 1] = f ** (t + P - k)
        decay[:, h, 2] = b ** (k + P - t)
    put("decay", decay * HD ** -0.5)

    def angles(dim):
        inv = (1.0 / (np.float32(10000.0) ** (np.arange(0, dim, 2, dtype=np.float32) / np.float32(dim)))).astype(np.float32)
        a = (np.arange(SEQ, dtype=np.float32)[:, None] * inv[None, :]).astype(np.float64)
        return a.reshape(MT, P, dim // 2).transpose(1, 0, 2)

    put("rcos", np.cos(angles(HD)))
    put("rsin", np.sin(angles(HD)))
    put("mcos", np.cos(angles(ROPE)))
    put("msin", np.sin(angles(ROPE)))
    put("mnsin", -np.sin(angles(ROPE)))
    band = np.zeros((4, SEQ, SEQ))
    for g, w in enumerate(POOL_WINDOWS):
        for tt in range(SEQ):
            a, b = max(tt - w // 2, 0), min(tt + w // 2, SEQ)
            band[g, a:b, tt] = 1.0 / (b - a)
            band[g, tt, tt] -= 1.0
    cut = np.zeros((P, 4, MT, POOL_REACH))
    cut[:, :, 0] = band[:, 0:P, 0:POOL_REACH].transpose(1, 0, 2)
    cut[:, :, 1] = band[:, P:, SEQ - POOL_REACH:].transpose(1, 0, 2)
    put("band", cut)
    return c.astype(np.float32)


def lay_out(a):
    import numpy as np

    widths = (512, 512, 512, 512, 256, 256, 512, 512, 16, 16, 512, 512, 512, 256, 64, 512)
    names = ("rq", "rk", "rv", "rg", "gq", "gk", "gv", "gg", "af", "ab", "pv", "pg", "mq", "mkv", "mkr", "mg")
    at = dict(zip(names, np.cumsum((0,) + widths[:-1])))
    wide = dict(zip(names, widths))
    parts = {"lat": ("mkv", "af", "ab", "mkr"), "gqk": ("gq", "gk")}
    y_rows = [g * GROUP_W for g in (3, 2, 1, 0)]
    stream = np.zeros((DEPTH, GRANULES, P, 2, 512), np.float32)
    for l in range(DEPTH):
        j = 0
        for name, width, src, base, n_slots, per in STAGES:
            if name.startswith("out"):
                c = int(name[3:])
                w = np.concatenate([a["w_out"][l, r:r + GROUP_W, c * 512:(c + 1) * 512] for r in y_rows])
            elif name.startswith("wq"):
                w = a["mla_wq_b"][l][:, int(name[2:]) * width:(int(name[2:]) + 1) * width]
            elif name.startswith("wkv"):
                w = a["mla_wkv_b"][l][:, int(name[3:]) * width:(int(name[3:]) + 1) * width]
            else:
                w = np.concatenate([a["w_in"][l][:, at[n]:at[n] + wide[n]] for n in parts.get(name, (name,))], axis=1)
            w = w.reshape(n_slots // per, per, P, width)
            stream[l, j:j + n_slots // per, :, 0:per, 0:width] = w.transpose(0, 2, 1, 3)
            j += n_slots // per
    stream = stream.reshape(DEPTH, PER_RING, RING, P, GRAN)

    def columns(v):
        return v.reshape(-1, P).T

    gains = np.zeros((P, DEPTH, GAIN_W), np.float32)
    mats = np.zeros((DEPTH, P, MAT_W), np.float32)
    for l in range(DEPTH):
        gains[:, l] = np.concatenate([
            columns(a["norm_g"][l]), np.ones((P, GT), np.float32), columns(a["pool_scale"][l]),
            columns(a["gla_norm_g"][l]), columns(a["ret_norm_g"][l]), columns(a["mla_q_norm_g"][l]),
            columns(a["mla_kv_norm_g"][l]), columns(a["mla_qk_norm_q"][l][:NOPE]),
            columns(a["mla_qk_norm_k"][l][:NOPE])], axis=1)
        mats[l, :, M_POOL:M_POOL + GROUP_W] = a["pool_w"][l].transpose(1, 0, 2).reshape(P, GROUP_W)
        for d, way in enumerate(("f", "b")):
            to = slice(M_WA + d * 256, M_WA + (d + 1) * 256)
            row = WA_ROW + d * GLA_RANK
            mats[l, row:row + GLA_RANK, to] = a[f"gla_wa2_{way}"][l]
            mats[l, WA_ROW + 2 * GLA_RANK, to] = a[f"gla_ba_{way}"][l]
        mats[l, :, M_ROPE:M_ROPE + ROPE] = a["mla_qk_norm_q"][l][NOPE:]
        mats[l, :, M_ROPE + ROPE:] = a["mla_qk_norm_k"][l][NOPE:]
    return {"x_in": a["x"].reshape(SEQ, D_MODEL), "stream": stream, "mats_in": mats,
            "gains_in": gains.reshape(P, DEPTH * GAIN_W), "consts_in": shape_constants()}


def kernel(**inputs):
    import numpy as np
    import concourse.bacc as bacc
    from concourse.bass_utils import run_bass_kernel_spmd

    arrays = lay_out({n: np.asarray(v) for n, v in inputs.items()})
    arrays = {n: np.ascontiguousarray(v) for n, v in arrays.items()}
    nc = bacc.Bacc("TRN2", target_bir_lowering=False, num_devices=1)
    args = [nc.dram_tensor(n, v.shape, F32, kind="ExternalInput").ap() for n, v in arrays.items()]
    out = nc.dram_tensor("out", (SEQ, D_MODEL), F32, kind="ExternalOutput").ap()
    build(nc, *args, out)
    result = run_bass_kernel_spmd(nc, [arrays], core_ids=[0])
    return result.results[0]["out"].reshape(1, SEQ, D_MODEL)
```

```python
from contextlib import ExitStack

import concourse.bass as bass
from concourse import mybir

F32 = mybir.dt.float32
F32R = mybir.dt.float32r
I32 = mybir.dt.int32
ALU = mybir.AluOpType
ACT = mybir.ActivationFunctionType
AX_X = mybir.AxisListType.X

P = 128
D_MODEL, SEQ, DEPTH = 2048, 256, 2
MT = SEQ // P
KT = D_MODEL // P
GROUP_W = D_MODEL // 4
HEADS = 4
HD = GROUP_W // HEADS
GT = GROUP_W // P
EPS = 1e-6
GLA_DK, GLA_RANK, GLA_TAU, GLA_CHUNK = 64, 16, 16.0, 64
POOL_WINDOWS = (2, 4, 8, 16)
POOL_REACH = P + max(POOL_WINDOWS) // 2
NOPE, ROPE, Q_RANK, KV_RANK = 128, 64, 512, 256
QK_W = NOPE + ROPE
LAT_W = KV_RANK + 2 * GLA_RANK + ROPE
WA_ROW = 32

RING = 4
POOL_SPLITS = 3
GRAN = 2 * 512

SLOT = {"D": 0, "C": GT, "B": 2 * GT, "A": 3 * GT}

STAGES = {}
for n_, w_ in (("mq", 512), ("lat", LAT_W), ("mg", 512), ("pv", 512), ("pg", 512), ("gqk", 512),
               ("gv", 512), ("gg", 512), ("rq", 512), ("rk", 512), ("rv", 512), ("rg", 512)):
    STAGES[n_] = (w_, "x", 0, KT, 2)
for i_ in range(2):
    STAGES[f"wq{i_}"] = (2 * QK_W, "y", SLOT["B"], Q_RANK // P, 2)
    STAGES[f"wkv{i_}"] = (512, "y", SLOT["A"], KV_RANK // P, 1)
for i_ in range(4):
    STAGES[f"out{i_}"] = (512, "y", 0, KT, 2)
ORDER = ([("mq", 8), ("lat", 8), ("mg", 8), ("pv", 2), ("wq0", 2), ("pv", 2), ("wq1", 2), ("pv", 2),
          ("wkv0", 2), ("pv", 1), ("wkv1", 2), ("pv", 1)]
         + [(n_, 8) for n_ in ("pg", "gqk", "gv", "gg", "rq", "rk", "rv", "rg", "out0", "out1", "out2", "out3")])
PAIR = {n_: i_ % 2 for i_, n_ in enumerate(
    ("mq", "lat", "mg", "pv", "pg", "gqk", "gv", "gg", "rq", "rk", "rv", "rg", "out0", "out1", "out2", "out3"))}
PAIR.update({n_: 0 for n_ in ("wq0", "wq1", "wkv0", "wkv1")})
PLAN, END, NTH = [], {}, {}
done_, used_ = {}, [0, 0]
for n_, count_ in ORDER:
    w_, t_, b_, k_, per_ = STAGES[n_]
    if n_ not in done_:
        done_[n_], NTH[n_] = 0, used_[PAIR[n_]]
        used_[PAIR[n_]] += 1
    for _ in range(count_):
        PLAN.append((n_, [b_ + per_ * done_[n_] + i_ for i_ in range(per_)]))
        done_[n_] += 1
    END[n_] = len(PLAN)
PAIR_USES = tuple(used_)
GRANULES = len(PLAN)
PER_RING = GRANULES // RING
assert GRANULES % RING == 0

CONSTS, nc_ = {}, 0
for n_, w_ in (("ident", P), ("tri_f", P), ("tri_b", P), ("after", P), ("before", P),
               ("decay", HEADS * 3 * P), ("rcos", MT * HD // 2), ("rsin", MT * HD // 2),
               ("mcos", MT * ROPE // 2), ("msin", MT * ROPE // 2), ("mnsin", MT * ROPE // 2),
               ("band", 4 * MT * POOL_REACH)):
    CONSTS[n_] = (nc_, w_)
    nc_ += w_
CONST_W = nc_
G_NORM, G_Y, G_QN, G_KVN, G_QK = 0, KT, 2 * KT, 2 * KT + 4, 2 * KT + 6
GAIN_W = 2 * KT + 8
M_POOL, M_WA, M_ROPE = 0, GROUP_W, 2 * GROUP_W
MAT_W = 2 * GROUP_W + 2 * ROPE


class Signal:

    def __init__(self, sem, per_layer, primed):
        self.sem, self.per_layer, self.primed = sem, per_layer, primed

    def at(self, l, n):
        return self.sem, l * self.per_layer + (n + self.primed)


def build(nc, x_in, stream, mats_in, gains_in, consts_in, out):
    with ExitStack() as ctx:
        def sb(name, shape, dt=F32):
            return ctx.enter_context(nc.sbuf_tensor(name, shape, dt))

        def signal(name, per_layer, primed=0):
            return Signal(ctx.enter_context(nc.semaphore(name)), per_layer, primed)

        raw = [sb(f"raw{r}", [P, GRAN]) for r in range(RING)]
        hi = [sb(f"hi{r}", [P, GRAN], F32R) for r in range(RING)]
        lo = [sb(f"lo{r}", [P, GRAN], F32R) for r in range(RING)]
        xT_hi = sb("xT_hi", [P, KT, SEQ], F32R)
        xT_lo = sb("xT_lo", [P, KT, SEQ], F32R)
        yT_hi = sb("yT_hi", [P, KT, SEQ], F32R)
        yT_lo = sb("yT_lo", [P, KT, SEQ], F32R)
        x = sb("x", [P, MT, D_MODEL])
        consts = sb("consts", [P, CONST_W])
        gains_all = sb("gains_all", [P, (DEPTH + 1) * GAIN_W])
        gains = sb("gains", [P, GAIN_W])
        mats = sb("mats", [P, MAT_W])
        rope_tab = sb("rope_tab", [P, 2, 2, MT, ROPE])
        gate0 = sb("gate0", [P, MT, GROUP_W])
        gate1 = sb("gate1", [P, MT, GROUP_W])
        aT = sb("aT", [P, MT, P])
        q_heads = sb("q_heads", [P, 2, 2, MT, 2, P])
        k_dec = sb("k_dec", [P, 2, HEADS, P])
        keep_bits = sb("keep_bits", [P, 2, P], I32)
        work = sb("work", [P, 8448])
        stat = sb("stat", [P, 64])

        def const(name):
            at, w = CONSTS[name]
            return consts[:, at:at + w]

        def area(at, width, pattern=None, **sizes):
            v = work[:, at:at + width]
            return v.rearrange(pattern, **sizes) if pattern else v

        zq = area(0, 1024, "p (m c) -> p m c", m=MT)
        zlat = area(1024, MT * LAT_W, "p (m c) -> p m c", m=MT)
        qr = area(1792, 512, "p (m h c) -> p m h c", m=MT, h=HEADS)
        q_sb = area(2304, 1536, "p (m h c) -> p m h c", m=MT, h=HEADS)
        probs = area(1792, 2048, "p (m h j) -> p m h j", m=MT, h=HEADS)
        kv_sb = area(3840, 2048, "p (m h c) -> p m h c", m=MT, h=HEADS)
        kr = area(5888, 512, "p (m h c) -> p m h c", m=MT, h=HEADS)
        sq_q = [area(0, 768), area(6400, 768)]
        sq_k = [area(0, 512), area(7936, 512)]
        rot_d = area(7424, 512, "p (m h c) -> p m h c", m=MT, h=HEADS)
        kpe = area(768, 128, "p (m c) -> p m c", m=MT)
        kpe_x = area(896, 128, "p (m c) -> p m c", m=MT)
        probsT = area(512, 1024, "p (b j t) -> p b j t", b=2, j=MT)
        u = area(6400, 1024, "p (m c) -> p m c", m=MT)
        pooledT = area(7424, 1024, "p (g t) -> p g t", g=4)
        zb = area(0, 1024, "p (m a c) -> p m a c", m=MT, a=2)
        v_b = area(1024, 1024, "p (m c) -> p m c", m=MT)
        la = area(2048, 1024, "p (m c) -> p m c", m=MT)
        score_b = area(2048, 1024, "p (m h i) -> p m h i", m=MT, h=HEADS)
        e_pos = area(3072, 1024, "p (d f t) -> p d f t", d=2, f=2)
        e_neg = area(4096, 1024, "p (d f t) -> p d f t", d=2, f=2)
        sq_b = area(4096, 512)
        e_rem = area(5120, 1024, "p (m d c) -> p m d c", m=MT, d=2)
        picked = area(7680, 512, "p (h i) -> p h i", h=HEADS)
        state = area(6144, 1536, "p (d n a e) -> p d n a e", d=2, n=3, a=2)
        rq_rot = area(0, 1024, "p (n c) -> p n c", n=MT * HEADS)
        rk_rot = area(1024, 1024, "p (n c) -> p n c", n=MT * HEADS)
        score_a = area(0, 2048, "p (h j t) -> p h j t", h=HEADS, j=MT)
        qT_a = area(2048, 1024, "p (h t) -> p h t", h=HEADS)
        rot_a = area(3072, 1024, "p (n c) -> p n c", n=MT * HEADS)
        sq_a = area(3072, 512)
        kT_a = area(4096, 1024, "p (h t) -> p h t", h=HEADS)
        z_rk = area(5120, 1024, "p (m c) -> p m c", m=MT)
        v_a = area(6144, 1024, "p (m c) -> p m c", m=MT)

        cols, cols_d = iter(range(64)), iter(range(1728, 1792))

        def stats(n):
            at = [next(cols) for _ in range(n)][0]
            return stat[:, at:at + n]

        def stats_d(n):
            at = [next(cols_d) for _ in range(n)][0]
            return work[:, at:at + n]

        x_sq = stats(MT * 4).rearrange("p (m c) -> p m c", m=MT)
        x_ms, x_rs = stats(MT), stats(MT)
        lq_sq, lq_ms, lq_rs = stats(MT), stats(MT), stats(MT)
        lk_sq, lk_ms, lk_rs, kpe_sq = stats(MT), stats(MT), stats(MT), stats(MT)
        q_sq, q_rs, k_sq, k_rs = stats_d(8), stats_d(8), stats_d(8), stats_d(8)
        q_ms, k_ms = q_sq, k_sq
        top, neg_top, p_sum, p_inv = stats_d(8), stats_d(8), stats_d(8), stats_d(8)
        o_sq, o_ms, o_rs = stats(8), stats(8), stats(8)
        minus_half = stats(8)
        table_loader = stats(1)

        pair = [[ctx.enter_context(nc.psum_tensor(f"pair{a}{m}", [P, 512], F32)) for m in range(MT)]
                for a in range(2)]
        bank = [ctx.enter_context(nc.psum_tensor(f"bank{b}", [P, 512], F32)) for b in range(4)]

        loaded = [signal(f"loaded{r}", 16 * PER_RING) for r in range(RING)]
        rounded = [signal(f"rounded{r}", PER_RING) for r in range(RING)]
        split = [signal(f"split{r}", PER_RING, primed=1) for r in range(RING)]
        multiplied = [signal(f"multiplied{r}", PER_RING, primed=1) for r in range(RING)]
        taken = [signal(f"taken{a}", MT * PAIR_USES[a], primed=1) for a in range(2)]
        x_loaded = [signal(f"x_loaded{c}", 0) for c in range(4)]
        ident_loaded = signal("ident_loaded", 0)
        gains_loaded = signal("gains_loaded", 0)
        consts_loaded = signal("consts_loaded", 0)
        mats_loaded = signal("mats_loaded", 16)
        stored = signal("stored", 0)
        cleared = signal("cleared", 0)
        bits_ready = signal("bits_ready", 2)
        added = [signal(f"added{c}", MT, primed=1) for c in range(4)]
        gains_ready = signal("gains_ready", 1)
        half_out = signal("half_out", 4)
        act_step = signal("act_step", 4)
        dve_step = signal("dve_step", 24)
        tabs_ready = signal("tabs_ready", 6)
        x_filled, xT_rounded, xT_ready = signal("x_filled", 8), signal("xT_rounded", KT), signal("xT_ready", KT)
        x_squared, x_ms_ready, x_rs_ready = signal("x_squared", 8), signal("x_ms_ready", 1), signal("x_rs_ready", 1)
        zq_ready, zlat_ready = signal("zq_ready", MT), signal("zlat_ready", MT)
        lq_squared, lq_ms_ready, lq_rs_ready = signal("lq_squared", MT), signal("lq_ms_ready", 1), signal("lq_rs_ready", 1)
        lk_squared, lk_ms_ready, lk_rs_ready = signal("lk_squared", 2 * MT), signal("lk_ms_ready", 1), signal("lk_rs_ready", 1)
        lq_filled, lqT_rounded, lqT_ready = signal("lq_filled", 2), signal("lqT_rounded", 4), signal("lqT_ready", 4)
        lk_filled, lkT_rounded, lkT_ready = signal("lk_filled", 1), signal("lkT_rounded", 2), signal("lkT_ready", 2)
        aT_filled, aT_ready = signal("aT_filled", 1), signal("aT_ready", 1)
        gate0_ready, gate1_ready = signal("gate0_ready", 2 * MT), signal("gate1_ready", 2 * MT)
        q_ready, kv_ready = signal("q_ready", 2 * MT), signal("kv_ready", 2 * MT)
        q_squared, q_ms_ready, q_rs_ready = signal("q_squared", MT), signal("q_ms_ready", 1), signal("q_rs_ready", 1)
        k_squared, k_ms_ready, k_rs_ready = signal("k_squared", MT), signal("k_ms_ready", 1), signal("k_rs_ready", 1)
        q_sq_read = signal("q_sq_read", 4)
        ob_sq_read, oa_sq_read = signal("ob_sq_read", 2), signal("oa_sq_read", 2)
        q_scaled, k_scaled = signal("q_scaled", MT), signal("k_scaled", 1)
        q_turned, k_turned = signal("q_turned", 1), signal("k_turned", 1)
        tq_filled, qT_rounded, qT_ready = signal("tq_filled", 2), signal("qT_rounded", 2), signal("qT_ready", 2)
        tk_filled, kT_rounded, kT_ready = signal("tk_filled", 2), signal("kT_rounded", 2), signal("kT_ready", 2)
        tr_filled, qr_rounded, kr_rounded = signal("tr_filled", 2), signal("qr_rounded", 2), signal("kr_rounded", 4)
        qr_ready, kr_ready = signal("qr_ready", 2), signal("kr_ready", 4)
        sd_filled, top_ready, probs_ready = signal("sd_filled", 4), signal("top_ready", 4), signal("probs_ready", 8)
        inv_ready = signal("inv_ready", 1)
        pt_filled, probsT_ready, pv_done = signal("pt_filled", 4), signal("probsT_ready", 4), signal("pv_done", 4)
        yD_ready, yD_filled = signal("yD_ready", 8), signal("yD_filled", 2)
        yTD_rounded, yTD_ready = signal("yTD_rounded", 4), signal("yTD_ready", 4)
        u_ready, cp_filled, pooled_ready = signal("u_ready", MT), signal("cp_filled", 2), signal("pooled_ready", 2)
        cm_filled, yC_ready, yC_filled = signal("cm_filled", 2, primed=1), signal("yC_ready", 2), signal("yC_filled", 2)
        yTC_rounded, yTC_ready = signal("yTC_rounded", 4), signal("yTC_ready", 4)
        zb_ready, v_b_ready = signal("zb_ready", MT), signal("v_b_ready", MT)
        la_filled, soft_ready, la_ready = signal("la_filled", 2), signal("soft_ready", 2), signal("la_ready", 2, primed=1)
        cum_filled, e_ready = signal("cum_filled", 2), signal("e_ready", 4)
        rem_filled, e_rem_ready = signal("rem_filled", 2), signal("e_rem_ready", 2)
        tb_filled, q_b_ready, k_b_ready = signal("tb_filled", 2), signal("q_b_ready", 4), signal("k_b_ready", 2)
        k_dec_ready = signal("k_dec_ready", 4)
        sb_filled, picked_ready, score_b_ready = signal("sb_filled", 4), signal("picked_ready", 4), signal("score_b_ready", 2, primed=1)
        kv_filled, kv_kept, state_ready = signal("kv_filled", 4), signal("kv_kept", 12), signal("state_ready", 8)
        ob_filled, ob_squared, ob_ms_ready, ob_rs_ready = (
            signal("ob_filled", 2), signal("ob_squared", 2), signal("ob_ms_ready", 1), signal("ob_rs_ready", 1))
        yB_ready, yB_filled = signal("yB_ready", 8), signal("yB_filled", 2)
        yTB_rounded, yTB_ready = signal("yTB_rounded", 4), signal("yTB_ready", 4)
        z_rq_ready, z_rk_ready, v_a_ready = signal("z_rq_ready", MT), signal("z_rk_ready", MT), signal("v_a_ready", MT)
        rq_turned, rk_turned = signal("rq_turned", 2), signal("rk_turned", 2)
        aq_filled, qT_a_ready = signal("aq_filled", 2), signal("qT_a_ready", 2)
        ak_filled, kT_a_ready = signal("ak_filled", 2), signal("kT_a_ready", 2)
        sa_filled, score_a_ready = signal("sa_filled", 4), signal("score_a_ready", 4)
        oa_filled, oa_squared, oa_ms_ready, oa_rs_ready = (
            signal("oa_filled", 2), signal("oa_squared", 2), signal("oa_ms_ready", 1), signal("oa_rs_ready", 1))
        yA_ready, yA_filled = signal("yA_ready", 8, primed=1), signal("yA_filled", 2)
        yTA_rounded, yTA_ready = signal("yTA_rounded", 4, primed=1), signal("yTA_ready", 4, primed=1)

        def bcast(ap, axis, n):
            shape = list(ap.shape)
            assert shape[axis] == 1
            shape[axis] = n
            return ap.broadcast_to(shape)

        def rotary(slot, i, half, tiles=yT_hi):
            return tiles[64 * half:64 * half + 64, slot + i:slot + 4:2, :]

        def bank_rows(b, i):
            return bank[b][64 * i:64 * i + 64, :].rearrange("p (f t) -> p f t", f=2)

        def per_head(s):
            return s.rearrange("p (m h o) -> p m h o", m=MT, o=1)

        block = ctx.enter_context(nc.Block())

        @block.sync
        def _(sp):
            sp.dma_start(x[:, :, 0:512], x_in.rearrange("(m p) (c n) -> c p m n", p=P, c=4)[0]
                         ).then_inc(x_loaded[0].sem, 16)
            with sp.Fori(0, DEPTH) as l:
                with sp.Fori(0, PER_RING) as k:
                    for r in range(RING):
                        sp.wait_ge(*split[r].at(l, k))
                        sp.dma_start(raw[r][:], stream[l, k, r]).then_inc(loaded[r].sem, 16)
            for c in range(4):
                for m in range(MT):
                    sp.wait_ge(*added[c].at(DEPTH - 1, m + 1))
                    sp.dma_start(out.rearrange("(m p) (c n) -> m c p n", p=P, c=4)[m, c],
                                 x[:, m, c * 512:(c + 1) * 512]).then_inc(stored.sem, 16)
            sp.wait_ge(stored.sem, 16 * 4 * MT)

        @block.tensor
        def _(pe):
            for sig in (*multiplied, cm_filled):
                pe.sem_inc(sig.sem, 1)
            pe.wait_ge(ident_loaded.sem, 16)
            ident = const("ident")

            with pe.Fori(0, DEPTH) as l:
                pos = [0]

                def granules(upto):
                    for j in range(pos[0], upto):
                        name, slots = PLAN[j]
                        width, src, base, n_slots, per = STAGES[name]
                        a, r = PAIR[name], j % RING
                        first = slots[0] == base
                        if first:
                            pe.wait_ge(*taken[a].at(l, MT * NTH[name]))
                        if name == "wq0" and first:
                            pe.wait_ge(*lqT_ready.at(l, 4))
                        if name == "wkv0" and first:
                            pe.wait_ge(*lkT_ready.at(l, 2))
                        if name == "out0" and slots[0] % GT == 0:
                            pe.wait_ge(*(yTD_ready, yTC_ready, yTB_ready, yTA_ready)[slots[0] // GT].at(l, 4))
                        t_hi, t_lo = (xT_hi, xT_lo) if src == "x" else (yT_hi, yT_lo)

                        def product(i, m, x_part, w_part, last=False):
                            return nc.tensor.matmul(
                                pair[a][m][:, 0:width], x_part[:, slots[i], m * P:(m + 1) * P],
                                w_part[r][:, i * 512:i * 512 + width],
                                start=(slots[i] == base and x_part is t_hi and w_part is hi), stop=last)

                        each = [(i, m) for i in range(per) for m in range(MT)]
                        if name == "mq":
                            pe.wait_ge(*rounded[r].at(l, j // RING + 1))
                            pe.wait_ge(*xT_rounded.at(l, slots[-1] + 1))
                            for i, m in each:
                                product(i, m, t_hi, hi)
                            pe.wait_ge(*xT_ready.at(l, slots[-1] + 1))
                        pe.wait_ge(*split[r].at(l, j // RING + 1))
                        ends = slots[-1] == base + n_slots - 1
                        if name.startswith("out") and ends:
                            each.sort(key=lambda im: im[1])
                        for i, m in each:
                            if name != "mq":
                                product(i, m, t_hi, hi)
                            product(i, m, t_hi, lo)
                            mm = product(i, m, t_lo, hi, last=ends and i == per - 1)
                            if name.startswith("out") and ends and (i, m) == (per - 1, 0):
                                mm.then_inc(half_out.sem, 1)
                        mm.then_inc(multiplied[r].sem, 1)
                    assert pos[0] <= upto
                    pos[0] = upto

                def turn(b, tiles):
                    for i, tile in enumerate(tiles):
                        t = nc.tensor.transpose(bank[b][:, i * P:(i + 1) * P], tile, ident)
                    return t

                def turn_x(f):
                    turn(f % 4, [x[:, m, kt * P:(kt + 1) * P] for kt in (2 * f, 2 * f + 1)
                                 for m in range(MT)]).then_inc(x_filled.sem, 1)

                for f in range(8):
                    if f == 0:
                        pe.wait_ge(*yA_ready.at(l, 0))
                    if f == 2:
                        pe.wait_ge(*yTA_ready.at(l, 0))
                    if f >= 4:
                        pe.wait_ge(*xT_ready.at(l, 2 * (f - 4) + 2))
                    if f % 2 == 0:
                        pe.wait_ge(x_loaded[f // 2].sem, 16)
                        pe.wait_ge(*added[f // 2].at(l, 0))
                    turn_x(f)
                    if f >= 1:
                        granules(f)
                granules(13)

                for f in range(2):
                    pe.wait_ge(*zq_ready.at(l, MT))
                    pe.wait_ge(*xT_ready.at(l, 10 + 2 * f))
                    turn(f, [zq[:, m, kt * P:(kt + 1) * P] for kt in (2 * f, 2 * f + 1)
                             for m in range(MT)]).then_inc(lq_filled.sem, 1)
                granules(19)
                pe.wait_ge(*zlat_ready.at(l, MT))
                pe.wait_ge(*xT_ready.at(l, KT))
                turn(2, [zlat[:, m, kt * P:(kt + 1) * P] for kt in range(2)
                         for m in range(MT)]).then_inc(lk_filled.sem, 1)
                turn(3, [zlat[:, m, KV_RANK - WA_ROW:KV_RANK - WA_ROW + P]
                         for m in range(MT)]).then_inc(aT_filled.sem, 1)
                granules(40)

                for f in range(2):
                    pe.wait_ge(*lqT_ready.at(l, 2 * f + 2))
                    pe.wait_ge(*q_scaled.at(l, MT))
                    turn(f, [q_sb[:, m, h, 0:NOPE] for h in (2 * f, 2 * f + 1)
                             for m in range(MT)]).then_inc(tq_filled.sem, 1)
                granules(44)
                pe.wait_ge(*q_turned.at(l, 1))
                pe.wait_ge(*qT_ready.at(l, 1))
                turn(0, [qr[:, m, 2 * a:2 * a + 2, :].rearrange("p h c -> p (h c)") for a in range(2)
                         for m in range(MT)]).then_inc(tr_filled.sem, 1)
                granules(46)
                for f in range(2):
                    pe.wait_ge(*(lkT_ready, aT_ready)[f].at(l, (2, 1)[f]))
                    pe.wait_ge(*k_scaled.at(l, 1))
                    turn(2 + f, [kv_sb[:, m, h, 0:NOPE] for h in (2 * f, 2 * f + 1)
                                 for m in range(MT)]).then_inc(tk_filled.sem, 1)
                granules(47)
                pe.wait_ge(*k_turned.at(l, 1))
                pe.wait_ge(*qT_ready.at(l, 2))
                turn(1, [kr[:, m, 2 * a:2 * a + 2, :].rearrange("p h c -> p (h c)") for a in range(2)
                         for m in range(MT)]).then_inc(tr_filled.sem, 1)
                granules(49)

                def scores_d(m):
                    for f in range(2):
                        b = (2 + 2 * m + f) % 4
                        if m == 0:
                            pe.wait_ge(*kT_ready.at(l, f + 1))
                        else:
                            pe.wait_ge(*(qr_ready, kr_ready)[f].at(l, (2, 4)[f]))
                        if m == 0 and f == 0:
                            pe.wait_ge(*qT_ready.at(l, 2))
                            pe.wait_ge(*kT_ready.at(l, 2))
                            pe.wait_ge(*qr_ready.at(l, 2))
                            pe.wait_ge(*kr_ready.at(l, 4))
                        for i, h in enumerate((2 * f, 2 * f + 1)):
                            acc = bank[b][:, i * SEQ:(i + 1) * SEQ]
                            q_hi = yT_hi[:, SLOT["B"] + h, m * P:(m + 1) * P]
                            q_lo = yT_lo[:, SLOT["B"] + h, m * P:(m + 1) * P]
                            k_hi, k_lo = yT_hi[:, SLOT["A"] + h, :], yT_lo[:, SLOT["A"] + h, :]
                            nc.tensor.matmul(acc, q_hi, k_hi, start=True, stop=False)
                            nc.tensor.matmul(acc, q_hi, k_lo, start=False, stop=False)
                            nc.tensor.matmul(acc, q_lo, k_hi, start=False, stop=False)
                            nc.tensor.matmul(acc, yT_hi[:, SLOT["D"] + h, m * P:(m + 1) * P],
                                             yT_hi[:, SLOT["C"] + h, :], start=False, stop=False)
                            mm = nc.tensor.matmul(acc, yT_hi[:, SLOT["D"] + h, m * P:(m + 1) * P],
                                                  yT_lo[:, SLOT["C"] + h, :], start=False, stop=True)
                        mm.then_inc(sd_filled.sem, 1)

                scores_d(0)
                granules(50)
                scores_d(1)
                granules(54)

                def turn_probs(h):
                    b = 2 + h % 2
                    if h < 2:
                        pe.wait_ge(*probs_ready.at(l, 8))
                    else:
                        pe.wait_ge(*probsT_ready.at(l, h - 1))
                    turn(b, [probs[:, m, h, j * P:(j + 1) * P] for j in range(MT)
                             for m in range(MT)]).then_inc(pt_filled.sem, 1)

                def times_v(h):
                    pe.wait_ge(*probsT_ready.at(l, h + 1))
                    for m in range(MT):
                        for j in range(MT):
                            mm = nc.tensor.matmul(bank[m][:, h * HD:(h + 1) * HD],
                                                  probsT[:, h % 2, j, m * P:(m + 1) * P],
                                                  kv_sb[:, j, h, NOPE:NOPE + HD],
                                                  start=(h == 0 and j == 0), stop=(h == 3 and j == 1),
                                                  skip_group_check=True)
                    mm.then_inc(pv_done.sem, 1)

                turn_probs(0)
                turn_probs(1)
                granules(55)
                times_v(0)
                times_v(1)
                turn_probs(2)
                turn_probs(3)
                granules(57)
                times_v(2)
                times_v(3)
                granules(61)

                def turn_y(b0, y, filled):
                    for f in range(2):
                        turn(b0 + f, [y[:, m, kt * P:(kt + 1) * P] for kt in (2 * f, 2 * f + 1)
                                      for m in range(MT)]).then_inc(filled.sem, 1)

                pe.wait_ge(*yD_ready.at(l, 8))
                pe.wait_ge(*probsT_ready.at(l, 4))
                turn_y(2, gate0, yD_filled)

                pe.wait_ge(*u_ready.at(l, MT))
                pe.wait_ge(consts_loaded.sem, 16)
                band = const("band").rearrange("p (g s t) -> p g s t", g=4, s=MT)
                for f in range(2):
                    for i, g in enumerate((2 * f, 2 * f + 1)):
                        acc = bank[f][:, i * SEQ:(i + 1) * SEQ]
                        nc.tensor.matmul(acc[:, 0:POOL_REACH], u[:, 0, g * P:(g + 1) * P], band[:, g, 0, :],
                                         start=True, stop=False, skip_group_check=True)
                        mm = nc.tensor.matmul(acc[:, SEQ - POOL_REACH:SEQ], u[:, 1, g * P:(g + 1) * P],
                                              band[:, g, 1, :], start=False, stop=True,
                                              skip_group_check=True)
                    mm.then_inc(cp_filled.sem, 1)
                granules(63)
                pe.wait_ge(*pooled_ready.at(l, 2))
                pe.wait_ge(*yTD_ready.at(l, 4))
                pe.wait_ge(*mats_loaded.at(l, 16))
                for m in range(MT):
                    for g in range(4):
                        mm = nc.tensor.matmul(bank[2 + m][:, g * P:(g + 1) * P],
                                              pooledT[:, g, m * P:(m + 1) * P],
                                              mats[:, M_POOL + g * P:M_POOL + (g + 1) * P],
                                              start=True, stop=True)
                    mm.then_inc(cm_filled.sem, 1)
                granules(65)
                pe.wait_ge(*yC_ready.at(l, 2))
                turn_y(0, gate1, yC_filled)

                pe.wait_ge(*aT_ready.at(l, 1))
                for m in range(MT):
                    nc.tensor.matmul(bank[2 + m][:], aT[:, m, :], mats[:, M_WA:M_WA + GROUP_W],
                                     start=True, stop=True).then_inc(la_filled.sem, 1)
                granules(72)
                pe.wait_ge(*la_ready.at(l, 2))
                pe.wait_ge(*yTC_ready.at(l, 4))
                for d, tri in enumerate(("tri_f", "tri_b")):
                    for f in range(2):
                        for m in range(MT):
                            at = d * 2 * P + f * P
                            mm = nc.tensor.matmul(bank[d][:, f * SEQ + m * P:f * SEQ + (m + 1) * P],
                                                  la[:, m, at:at + P], const(tri), start=True, stop=True)
                    mm.then_inc(cum_filled.sem, 1)
                for m in range(MT):
                    nc.tensor.matmul(bank[2 + m][:, 0:2 * P], const("after"), la[:, m, 0:2 * P],
                                     start=True, stop=True)
                    nc.tensor.matmul(bank[2 + m][:, 2 * P:4 * P], const("before"), la[:, m, 2 * P:4 * P],
                                     start=True, stop=True).then_inc(rem_filled.sem, 1)
                granules(75)
                pe.wait_ge(*zb_ready.at(l, MT))
                for a in range(2):
                    pe.wait_ge(*e_ready.at(l, 2 * a + 2))
                    turn(a, [zb[:, m, a, f * P:(f + 1) * P] for f in range(2)
                             for m in range(MT)]).then_inc(tb_filled.sem, 1)
                granules(79)

                def scores_b(m):
                    for d in range(2):
                        if m == 0:
                            pe.wait_ge(*e_rem_ready.at(l, d + 1))
                        for f in range(2):
                            mm = nc.tensor.matmul(
                                bank[(2 + 2 * m + d) % 4][:, f * SEQ:(f + 1) * SEQ],
                                e_neg[:, d, f, m * P:(m + 1) * P],
                                q_heads[:, d, f, m].rearrange("p i t -> p (i t)"), start=True, stop=True)
                        mm.then_inc(sb_filled.sem, 1)

                pe.wait_ge(*q_b_ready.at(l, 4))
                pe.wait_ge(*k_b_ready.at(l, 2))
                scores_b(0)
                scores_b(1)
                granules(81)

                def outer_kv(m):
                    pe.wait_ge(*k_dec_ready.at(l, 2 * m + 2))
                    pe.wait_ge(*picked_ready.at(l, 2 * m + 2))
                    for d in range(2):
                        for h in range(HEADS):
                            mm = nc.tensor.matmul(bank[(2 + 2 * m + d) % 4][:, h * HD:(h + 1) * HD],
                                                  k_dec[:, d, h], v_b[:, m, h * HD:(h + 1) * HD],
                                                  start=True, stop=True)
                        mm.then_inc(kv_filled.sem, 1)

                pe.wait_ge(*v_b_ready.at(l, MT))
                outer_kv(0)
                granules(82)
                outer_kv(1)
                granules(85)
                pe.wait_ge(*score_b_ready.at(l, 2))
                pe.wait_ge(*state_ready.at(l, 8))
                pe.wait_ge(*kv_kept.at(l, 12))
                for m in range(MT):
                    for h in range(HEADS):
                        nc.tensor.matmul(bank[m][:, h * HD:(h + 1) * HD], score_b[:, m, h, :],
                                         v_b[:, m, h * HD:(h + 1) * HD], start=(h == 0), stop=False,
                                         skip_group_check=True)
                    for c in range(2):
                        n = 2 * m + c
                        for h in range(HEADS):
                            for d in range(2):
                                t = n - 1 if d == 0 else 2 - n
                                if t < 0:
                                    continue
                                mm = nc.tensor.matmul(
                                    bank[m][c * 64:(c + 1) * 64, h * HD:(h + 1) * HD],
                                    q_heads[:, d, h // 2, m, h % 2, c * 64:(c + 1) * 64],
                                    state[:, d, t, h // 2, :], start=False, stop=True,
                                    skip_group_check=True)
                    mm.then_inc(ob_filled.sem, 1)
                granules(89)
                pe.wait_ge(*yB_ready.at(l, 8))
                turn_y(2, gate0, yB_filled)
                granules(92)

                pe.wait_ge(*rq_turned.at(l, 2))
                for f in range(2):
                    turn(f, [rq_rot[:, m * HEADS + h, :] for h in (2 * f, 2 * f + 1)
                             for m in range(MT)]).then_inc(aq_filled.sem, 1)
                granules(95)
                pe.wait_ge(*rk_turned.at(l, 2))
                pe.wait_ge(*yTB_ready.at(l, 4))
                for f in range(2):
                    turn(2 + f, [rk_rot[:, m * HEADS + h, :] for h in (2 * f, 2 * f + 1)
                                 for m in range(MT)]).then_inc(ak_filled.sem, 1)
                granules(98)
                for h in range(HEADS):
                    if h % 2 == 0:
                        pe.wait_ge(*qT_a_ready.at(l, h // 2 + 1))
                        pe.wait_ge(*kT_a_ready.at(l, h // 2 + 1))
                    if h == 1:
                        pe.wait_ge(*qT_a_ready.at(l, 2))
                    if h == 2:
                        pe.wait_ge(*kT_a_ready.at(l, 2))
                    for j in range(MT):
                        mm = nc.tensor.matmul(bank[h][:, j * SEQ:(j + 1) * SEQ],
                                              kT_a[:, h, j * P:(j + 1) * P], qT_a[:, h, :],
                                              start=True, stop=True)
                    mm.then_inc(sa_filled.sem, 1)
                granules(102)
                pe.wait_ge(*v_a_ready.at(l, MT))
                pe.wait_ge(*score_a_ready.at(l, 4))
                for m in range(MT):
                    for h in range(HEADS):
                        for j in range(MT):
                            mm = nc.tensor.matmul(bank[m][:, h * HD:(h + 1) * HD],
                                                  score_a[:, h, j, m * P:(m + 1) * P],
                                                  v_a[:, j, h * HD:(h + 1) * HD],
                                                  start=(h == 0 and j == 0), stop=(h == 3 and j == 1),
                                                  skip_group_check=True)
                    mm.then_inc(oa_filled.sem, 1)
                granules(109)
                pe.wait_ge(*yA_ready.at(l, 8))
                turn_y(2, gate1, yA_filled)
                granules(GRANULES)

        @block.scalar
        def _(act):
            act.dma_start(const("ident"), consts_in[:, 0:P]).then_inc(ident_loaded.sem, 16)
            act.dma_start(gains_all[:], gains_in).then_inc(gains_loaded.sem, 16)
            act.dma_start(x[:, :, 512:1024], x_in.rearrange("(m p) (c n) -> c p m n", p=P, c=4)[1]
                          ).then_inc(x_loaded[1].sem, 16)

            for sig in (*taken, yTA_rounded):
                act.sem_inc(sig.sem, 1)


            with act.Fori(0, DEPTH) as l:
                pos, step = [0], [0]

                def splits(upto):
                    for j in range(pos[0], upto):
                        r = j % RING
                        act.wait_ge(*loaded[r].at(l, 16 * (j // RING + 1)))
                        act.wait_ge(*multiplied[r].at(l, j // RING))
                        per, width = len(PLAN[j][1]), STAGES[PLAN[j][0]][0]
                        cut = [t[r][:].rearrange("p (i n) -> p i n", i=2)[:, 0:per, 0:width] for t in (hi, raw)]
                        nc.scalar.activation(cut[0], cut[1], ACT.Copy).then_inc(rounded[r].sem, 1)
                    assert pos[0] <= upto
                    pos[0] = upto

                def chained(ins):
                    step[0] += 1
                    ins.then_inc(act_step.sem, 1)
                    act.wait_ge(*act_step.at(l, step[0]))

                def stage_done(name):
                    act.wait_ge(*multiplied[(END[name] - 1) % RING].at(l, (END[name] - 1) // RING + 1))

                def take(name, dst, rs, ready, func=ACT.Copy, cols=512):
                    stage_done(name)
                    a = PAIR[name]
                    for m in range(MT):
                        nc.scalar.activation(dst(m), pair[a][m][:, 0:cols], func,
                                             scale=rs[:, m:m + 1]).then_inc(ready.sem, 1)
                    act.wait_ge(*ready.at(l, take_n[name]))
                    for m in range(MT):
                        act.sem_inc(taken[a].sem, 1)

                take_n = {"mq": 2, "lat": 2, "mg": 2, "wq0": 2, "wq1": 4, "wkv0": 2, "wkv1": 4, "pv": 2,
                          "pg": 2, "gqk": 2, "gv": 2, "gg": 4, "rq": 2, "rk": 2, "rv": 2, "rg": 4}

                def round_tiles(f0, filled, rounded_, dst, b0, gain, n_banks=2, slot0=0):
                    for f in range(n_banks):
                        act.wait_ge(*filled.at(l, f0 + f + 1))
                        for i in range(2):
                            kt = 2 * f + i
                            nc.scalar.activation(dst[:, slot0 + kt, :], bank[(b0 + f) % 4][:, i * SEQ:(i + 1) * SEQ],
                                                 ACT.Copy, scale=gains[:, gain + kt:gain + kt + 1]
                                                 ).then_inc(rounded_.sem, 1)

                def square_x(c):
                    act.wait_ge(x_loaded[c].sem, 16)
                    act.wait_ge(*added[c].at(l, 0))
                    if c > 0:
                        act.wait_ge(*x_squared.at(l, 2 * c))
                    for m in range(MT):
                        nc.scalar.activation(gate0[:, m, :], x[:, m, c * 512:(c + 1) * 512], ACT.Square,
                                             accum_out=x_sq[:, m, c:c + 1]).then_inc(x_squared.sem, 1)

                act.wait_ge(cleared.sem, 1)
                nc.scalar.activation(table_loader[:, 0:1], minus_half[:, 0:1], ACT.Copy)
                splits(1)
                act.wait_ge(*gains_ready.at(l, 1))
                for f in range(8):
                    splits(f + 1)
                    round_tiles(f, x_filled, xT_rounded, xT_hi, f % 4, G_NORM + 2 * f, n_banks=1, slot0=2 * f)
                    if f in (3, 5, 6):
                        square_x((3, 5, 6).index(f))
                splits(9)
                square_x(3)
                act.wait_ge(*cm_filled.at(l, 0))
                act.wait_ge(*la_ready.at(l, 0))
                act.dma_start(mats[:], mats_in[l]).then_inc(mats_loaded.sem, 16)
                splits(11)
                act.wait_ge(*x_rs_ready.at(l, 1))
                take("mq", lambda m: zq[:, m, :], x_rs, zq_ready)
                for m in range(MT):
                    nc.scalar.activation(gate0[:, m, :], zq[:, m, :], ACT.Square,
                                         accum_out=lq_sq[:, m:m + 1]).then_inc(lq_squared.sem, 1)
                splits(15)
                round_tiles(0, lq_filled, lqT_rounded, yT_hi, 0, G_QN, slot0=SLOT["B"])
                splits(18)
                take("lat", lambda m: zlat[:, m, :], x_rs, zlat_ready, cols=LAT_W)
                act.wait_ge(*lq_squared.at(l, MT))
                for m in range(MT):
                    nc.scalar.activation(gate0[:, m, 0:KV_RANK], zlat[:, m, 0:KV_RANK], ACT.Square,
                                         accum_out=lk_sq[:, m:m + 1]).then_inc(lk_squared.sem, 1)
                    nc.scalar.activation(gate0[:, m, 256:256 + ROPE], zlat[:, m, LAT_W - ROPE:LAT_W], ACT.Square,
                                         accum_out=kpe_sq[:, m:m + 1]).then_inc(lk_squared.sem, 1)
                splits(22)
                round_tiles(0, lk_filled, lkT_rounded, yT_hi, 2, G_KVN, n_banks=1, slot0=SLOT["A"])
                act.wait_ge(*aT_filled.at(l, 1))
                act.wait_ge(cleared.sem, 5)
                nc.scalar.activation(aT[32:64, :, :], bank[3][32:64, 0:MT * P].rearrange("p (m t) -> p m t", m=MT),
                                     ACT.Copy).then_inc(aT_ready.sem, 1)
                splits(26)
                act.wait_ge(*lk_squared.at(l, 2 * MT))
                take("mg", lambda m: gate0[:, m, :], x_rs, gate0_ready, func=ACT.Silu)
                splits(30)
                act.wait_ge(*lq_rs_ready.at(l, 1))
                take("wq0", lambda m: q_sb[:, m, 0:2, :].rearrange("p h c -> p (h c)"), lq_rs, q_ready, cols=2 * QK_W)
                splits(34)
                take("wq1", lambda m: q_sb[:, m, 2:4, :].rearrange("p h c -> p (h c)"), lq_rs, q_ready, cols=2 * QK_W)
                act.wait_ge(*q_ready.at(l, 4))
                for m in range(MT):
                    splits(35 + m)
                    nc.scalar.activation(sq_q[m], q_sb[:, m].rearrange("p h c -> p (h c)"), ACT.Square
                                         ).then_inc(q_squared.sem, 1)
                splits(38)
                act.wait_ge(*lk_rs_ready.at(l, 1))
                take("wkv0", lambda m: kv_sb[:, m, 0:2, :].rearrange("p h c -> p (h c)"), lk_rs, kv_ready)
                splits(41)
                take("wkv1", lambda m: kv_sb[:, m, 2:4, :].rearrange("p h c -> p (h c)"), lk_rs, kv_ready)
                for m in range(MT):
                    splits(41 + m)
                    act.wait_ge(*q_sq_read.at(l, 2))
                    nc.scalar.activation(sq_k[m].rearrange("p (h c) -> p h c", h=HEADS),
                                         kv_sb[:, m, :, 0:NOPE], ACT.Square).then_inc(k_squared.sem, 1)
                take("pv", lambda m: u[:, m, :], x_rs, u_ready)
                splits(43)
                for f in range(2):
                    act.wait_ge(*tq_filled.at(l, f + 1))
                    nc.scalar.activation(yT_hi[:, SLOT["B"] + 2 * f:SLOT["B"] + 2 * f + 2, :].rearrange("p h t -> p (h t)"),
                                         bank[f][:], ACT.Copy, scale=gains[:, G_QK:G_QK + 1]
                                         ).then_inc(qT_rounded.sem, 1)
                splits(46)
                act.wait_ge(*tr_filled.at(l, 1))
                for i in range(2):
                    nc.scalar.activation(rotary(SLOT["D"], i, i), bank_rows(0, i), ACT.Copy).then_inc(qr_rounded.sem, 1)
                splits(48)
                for f in range(2):
                    act.wait_ge(*tk_filled.at(l, f + 1))
                    nc.scalar.activation(yT_hi[:, SLOT["A"] + 2 * f:SLOT["A"] + 2 * f + 2, :].rearrange("p h t -> p (h t)"),
                                         bank[2 + f][:], ACT.Copy, scale=gains[:, G_QK + 1:G_QK + 2]
                                         ).then_inc(kT_rounded.sem, 1)
                splits(49)
                act.wait_ge(*tr_filled.at(l, 2))
                for i in range(2):
                    for half in (i, 1 - i):
                        nc.scalar.activation(rotary(SLOT["C"], i, half), bank_rows(1, i), ACT.Copy
                                             ).then_inc(kr_rounded.sem, 1)
                for m in range(MT):
                    splits(52 + m)
                    for f in range(2):
                        n = 2 * m + f
                        act.wait_ge(*top_ready.at(l, n + 1))
                        for i in range(2):
                            h = 2 * f + i
                            at = m * HEADS + h
                            nc.scalar.activation(probs[:, m, h, :], bank[(2 + n) % 4][:, i * SEQ:(i + 1) * SEQ],
                                                 ACT.Exp, bias=neg_top[:, at:at + 1], scale=QK_W ** -0.5,
                                                 accum_out=p_sum[:, at:at + 1]).then_inc(probs_ready.sem, 1)
                splits(54)
                take("pg", lambda m: gate1[:, m, :], x_rs, gate1_ready, func=ACT.Silu)
                splits(59)
                act.wait_ge(*pv_done.at(l, 4))
                take("gqk", lambda m: zb[:, m].rearrange("p a c -> p (a c)"), x_rs, zb_ready)
                splits(63)
                round_tiles(0, yD_filled, yTD_rounded, yT_hi, 2, G_Y + SLOT["D"], slot0=SLOT["D"])
                for f in range(2):
                    act.wait_ge(*cp_filled.at(l, f + 1))
                    nc.scalar.activation(pooledT[:, 2 * f:2 * f + 2, :].rearrange("p g t -> p (g t)"), bank[f][:],
                                         ACT.Copy).then_inc(pooled_ready.sem, 1)
                splits(67)
                round_tiles(0, yC_filled, yTC_rounded, yT_hi, 0, G_Y + SLOT["C"], slot0=SLOT["C"])
                for m in range(MT):
                    act.wait_ge(*la_filled.at(l, m + 1))
                    chained(nc.scalar.activation(la[:, m, :], bank[2 + m][:], ACT.Abs))
                splits(68)
                for m in range(MT):
                    chained(nc.scalar.activation(la[:, m, :], la[:, m, :], ACT.Exp, scale=-1.0))
                splits(69)
                for m in range(MT):
                    nc.scalar.activation(la[:, m, :], la[:, m, :], ACT.Ln, bias=1.0).then_inc(soft_ready.sem, 1)
                splits(71)
                take("gv", lambda m: v_b[:, m, :], x_rs, v_b_ready)
                splits(74)
                for d in range(2):
                    if d:
                        splits(75)
                    act.wait_ge(*cum_filled.at(l, d + 1))
                    for dst, sign in ((e_pos, 1.0), (e_neg, -1.0)):
                        nc.scalar.activation(dst[:, d].rearrange("p f t -> p (f t)"), bank[d][:], ACT.Exp,
                                             scale=sign / GLA_TAU).then_inc(e_ready.sem, 1)
                splits(76)
                for m in range(MT):
                    act.wait_ge(*rem_filled.at(l, m + 1))
                    nc.scalar.activation(e_rem[:, m].rearrange("p d c -> p (d c)"), bank[2 + m][:], ACT.Exp,
                                         scale=1.0 / GLA_TAU).then_inc(e_rem_ready.sem, 1)
                splits(77)
                act.wait_ge(*yD_filled.at(l, 2))
                take("gg", lambda m: gate0[:, m, :], x_rs, gate0_ready, func=ACT.Silu)
                splits(82)

                def keep(m):
                    for d in range(2):
                        act.wait_ge(*kv_filled.at(l, 2 * m + d + 1))
                        for c in range(2):
                            n = 2 * m + c
                            t = n if d == 0 else 3 - n
                            if t == 3:
                                continue
                            cut = bank[(2 + 2 * m + d) % 4][64 * c:64 * c + 64, :].rearrange(
                                "p (a i e) -> p a i e", a=2, i=2)
                            for i in range(2):
                                nc.scalar.activation(state[64 * i:64 * i + 64, d, t, :, :], cut[:, :, i, :], ACT.Copy
                                                     ).then_inc(kv_kept.sem, 1)

                keep(0)
                splits(84)
                keep(1)
                splits(84)
                act.wait_ge(*yC_filled.at(l, 2))
                take("rq", lambda m: gate1[:, m, :], x_rs, z_rq_ready)
                splits(87)
                for m in range(MT):
                    act.wait_ge(*ob_filled.at(l, m + 1))
                    if m:
                        act.wait_ge(*ob_sq_read.at(l, m))
                    nc.scalar.activation(sq_b, bank[m][:], ACT.Square).then_inc(ob_squared.sem, 1)
                splits(91)
                round_tiles(0, yB_filled, yTB_rounded, yT_hi, 2, G_Y + SLOT["B"], slot0=SLOT["B"])
                take("rk", lambda m: z_rk[:, m, :], x_rs, z_rk_ready)
                splits(94)
                for f in range(2):
                    act.wait_ge(*aq_filled.at(l, f + 1))
                    nc.scalar.activation(qT_a[:, 2 * f:2 * f + 2, :].rearrange("p h t -> p (h t)"), bank[f][:],
                                         ACT.Copy).then_inc(qT_a_ready.sem, 1)
                splits(97)
                for f in range(2):
                    act.wait_ge(*ak_filled.at(l, f + 1))
                    nc.scalar.activation(kT_a[:, 2 * f:2 * f + 2, :].rearrange("p h t -> p (h t)"), bank[2 + f][:],
                                         ACT.Copy).then_inc(kT_a_ready.sem, 1)
                splits(98)
                take("rv", lambda m: v_a[:, m, :], x_rs, v_a_ready)
                splits(104)
                for m in range(MT):
                    act.wait_ge(*oa_filled.at(l, m + 1))
                    if m:
                        act.wait_ge(*oa_sq_read.at(l, m))
                    nc.scalar.activation(sq_a, bank[m][:], ACT.Square).then_inc(oa_squared.sem, 1)
                splits(106)
                take("rg", lambda m: gate1[:, m, :], x_rs, gate1_ready, func=ACT.Silu)
                splits(111)
                round_tiles(0, yA_filled, yTA_rounded, yT_hi, 2, G_Y + SLOT["A"], slot0=SLOT["A"])
                splits(GRANULES)
                assert step[0] == act_step.per_layer, step[0]

        @block.vector
        def _(dve):
            for sig in (*split, *added, yA_ready, yTA_ready, la_ready, score_b_ready):
                dve.sem_inc(sig.sem, 1)
            dve.wait_ge(gains_loaded.sem, 16)
            nc.vector.tensor_copy(gains[:], gains_all[:, 0:GAIN_W]).then_inc(gains_ready.sem, 1)

            with dve.Fori(0, DEPTH) as l:
                pos, step = [POOL_SPLITS], [0]

                def splits(upto):
                    for j in range(pos[0], upto):
                        r = j % RING
                        dve.wait_ge(*rounded[r].at(l, j // RING + 1))
                        per, width = len(PLAN[j][1]), STAGES[PLAN[j][0]][0]
                        cut = [t[r][:].rearrange("p (i n) -> p i n", i=2)[:, 0:per, 0:width] for t in (lo, raw, hi)]
                        nc.vector.tensor_tensor(cut[0], cut[1], cut[2].bitcast(F32), ALU.subtract
                                                ).then_inc(split[r].sem, 1)
                    assert pos[0] <= upto
                    pos[0] = upto

                def chained(ins):
                    step[0] += 1
                    ins.then_inc(dve_step.sem, 1)
                    dve.wait_ge(*dve_step.at(l, step[0]))

                def lo_tiles(rounded_, ready, dst_hi, dst_lo, b0, gain, n_banks=2, slot0=0, r0=0):
                    for f in range(n_banks):
                        dve.wait_ge(*rounded_.at(l, r0 + 2 * f + 2))
                        for i in range(2):
                            kt = 2 * f + i
                            nc.vector.scalar_tensor_tensor(
                                out=dst_lo[:, slot0 + kt, :], in0=bank[(b0 + f) % 4][:, i * SEQ:(i + 1) * SEQ],
                                scalar=gains[:, gain + kt:gain + kt + 1], in1=dst_hi[:, slot0 + kt, :].bitcast(F32),
                                op0=ALU.mult, op1=ALU.subtract).then_inc(ready.sem, 1)

                def mean_square(sq, ms, width, ready):
                    nc.vector.tensor_scalar(ms, sq, 1.0 / width, EPS, ALU.mult, ALU.add).then_inc(ready.sem, 1)

                for f in range(8):
                    splits(max(POOL_SPLITS, f + 1))
                    dve.wait_ge(*gains_ready.at(l, 1))
                    lo_tiles(xT_rounded, xT_ready, xT_hi, xT_lo, f % 4, G_NORM + 2 * f, n_banks=1, slot0=2 * f, r0=2 * f)
                splits(10)
                dve.wait_ge(*x_squared.at(l, 8))
                chained(nc.vector.tensor_reduce(x_ms, x_sq, AX_X, ALU.add))
                mean_square(x_ms, x_ms, D_MODEL, x_ms_ready)
                splits(13)
                dve.wait_ge(*lq_squared.at(l, MT))
                mean_square(lq_sq, lq_ms, Q_RANK, lq_ms_ready)
                splits(15)
                lo_tiles(lqT_rounded, lqT_ready, yT_hi, yT_lo, 0, G_QN, slot0=SLOT["B"])
                dve.wait_ge(consts_loaded.sem, 16)
                dve.wait_ge(*score_b_ready.at(l, 0))
                for d, tri in enumerate(("tri_f", "tri_b")):
                    nc.vector.tensor_scalar(keep_bits[:, d, :], const(tri), -1.0, None, ALU.mult
                                            ).then_inc(bits_ready.sem, 1)
                splits(20)
                dve.wait_ge(*lk_squared.at(l, 2 * MT))
                mean_square(lk_sq, lk_ms, KV_RANK, lk_ms_ready)
                splits(22)
                lo_tiles(lkT_rounded, lkT_ready, yT_hi, yT_lo, 2, G_KVN, n_banks=1, slot0=SLOT["A"])
                for m in range(MT):
                    splits(36 + m)
                    dve.wait_ge(*q_squared.at(l, m + 1))
                    nc.vector.tensor_reduce(q_sq[:, m * HEADS:(m + 1) * HEADS],
                                            sq_q[m].rearrange("p (h c) -> p h c", h=HEADS), AX_X, ALU.add
                                            ).then_inc(q_sq_read.sem, 1)
                dve.wait_ge(*q_sq_read.at(l, 2))
                mean_square(q_sq, q_ms, QK_W, q_ms_ready)
                splits(39)
                dve.wait_ge(*q_rs_ready.at(l, 1))
                for m in range(MT):
                    splits(39 + m)
                    nc.vector.tensor_tensor(q_sb[:, m], q_sb[:, m], bcast(per_head(q_rs)[:, m], 2, QK_W), ALU.mult
                                            ).then_inc(q_scaled.sem, 1)
                splits(41)
                dve.wait_ge(*q_scaled.at(l, 2))
                dve.wait_ge(*tabs_ready.at(l, 6))
                half = ROPE // 2

                def table(which, part, n):
                    return bcast(rope_tab[:, which, part].rearrange("p m (o c) -> p m o c", o=1), 2, n)

                chained(nc.vector.tensor_tensor(qr[:], q_sb[:, :, :, NOPE:], table(0, 0, HEADS), ALU.mult))
                for a in range(2):
                    chained(nc.vector.tensor_tensor(
                        rot_d[:, :, :, a * half:(a + 1) * half],
                        q_sb[:, :, :, NOPE + (1 - a) * half:NOPE + (2 - a) * half],
                        table(0, 1, HEADS)[:, :, :, a * half:(a + 1) * half], ALU.mult))
                nc.vector.tensor_tensor(qr[:], qr[:], rot_d[:], ALU.add).then_inc(q_turned.sem, 1)
                for m in range(MT):
                    splits(42 + m)
                    dve.wait_ge(*k_squared.at(l, m + 1))
                    nc.vector.tensor_reduce(k_sq[:, m * HEADS:(m + 1) * HEADS],
                                            sq_k[m].rearrange("p (h c) -> p h c", h=HEADS), AX_X,
                                            ALU.add).then_inc(q_sq_read.sem, 1)
                splits(44)
                for m in range(MT):
                    dve.wait_ge(*q_sq_read.at(l, 4))
                    at = k_sq[:, m * HEADS:(m + 1) * HEADS]
                    chained(nc.vector.tensor_scalar(at, at, kpe_sq[:, m:m + 1], None, ALU.add))
                mean_square(k_sq, k_ms, QK_W, k_ms_ready)

                def lo_pair(rounded_, ready, b0, slot0, gain):
                    for f in range(2):
                        dve.wait_ge(*rounded_.at(l, f + 1))
                        at = slice(slot0 + 2 * f, slot0 + 2 * f + 2)
                        nc.vector.scalar_tensor_tensor(
                            out=yT_lo[:, at, :].rearrange("p h t -> p (h t)"), in0=bank[b0 + f][:],
                            scalar=gains[:, gain:gain + 1],
                            in1=yT_hi[:, at, :].rearrange("p h t -> p (h t)").bitcast(F32),
                            op0=ALU.mult, op1=ALU.subtract).then_inc(ready.sem, 1)

                lo_pair(qT_rounded, qT_ready, 0, SLOT["B"], G_QK)
                splits(45)
                dve.wait_ge(*k_rs_ready.at(l, 1))
                nc.vector.tensor_tensor(kv_sb[:, :, :, 0:NOPE], kv_sb[:, :, :, 0:NOPE], bcast(per_head(k_rs), 3, NOPE),
                                        ALU.mult).then_inc(k_scaled.sem, 1)
                splits(46)
                zpe = zlat[:, :, LAT_W - ROPE:LAT_W]
                chained(nc.vector.tensor_tensor(kpe[:], zpe, rope_tab[:, 1, 0], ALU.mult))
                for a in range(2):
                    chained(nc.vector.tensor_tensor(kpe_x[:, :, a * half:(a + 1) * half],
                                                    zpe[:, :, (1 - a) * half:(2 - a) * half],
                                                    rope_tab[:, 1, 1, :, a * half:(a + 1) * half], ALU.mult))
                chained(nc.vector.tensor_tensor(kpe[:], kpe[:], kpe_x[:], ALU.add))
                nc.vector.tensor_tensor(kr[:], bcast(kpe[:].rearrange("p m (o c) -> p m o c", o=1), 2, HEADS),
                                        bcast(per_head(k_rs), 3, ROPE), ALU.mult).then_inc(k_turned.sem, 1)

                splits(47)
                dve.wait_ge(*qr_rounded.at(l, 2))
                for i in range(2):
                    nc.vector.tensor_tensor(rotary(SLOT["D"], i, 1 - i), bank_rows(0, i),
                                            rotary(SLOT["D"], i, i).bitcast(F32), ALU.subtract
                                            ).then_inc(qr_ready.sem, 1)
                splits(48)
                lo_pair(kT_rounded, kT_ready, 2, SLOT["A"], G_QK + 1)
                splits(49)
                dve.wait_ge(*kr_rounded.at(l, 4))
                for i in range(2):
                    for half in (i, 1 - i):
                        nc.vector.tensor_tensor(rotary(SLOT["C"], i, half, yT_lo), bank_rows(1, i),
                                                rotary(SLOT["C"], i, i).bitcast(F32), ALU.subtract
                                                ).then_inc(kr_ready.sem, 1)
                for m in range(MT):
                    splits(52 + m)
                    for f in range(2):
                        n = 2 * m + f
                        dve.wait_ge(*sd_filled.at(l, n + 1))
                        at = slice(2 * n, 2 * n + 2)
                        chained(nc.vector.tensor_reduce(top[:, at], bank[(2 + n) % 4][:].rearrange("p (h j) -> p h j", h=2),
                                                        AX_X, ALU.max))
                        nc.vector.tensor_scalar(neg_top[:, at], top[:, at], -QK_W ** -0.5, None, ALU.mult
                                                ).then_inc(top_ready.sem, 1)
                splits(55)
                dve.wait_ge(*probs_ready.at(l, 8))
                nc.vector.reciprocal(p_inv, p_sum).then_inc(inv_ready.sem, 1)

                def keep_probsT(h):
                    dve.wait_ge(*pt_filled.at(l, h + 1))
                    if h >= 2:
                        dve.wait_ge(*pv_done.at(l, h - 1))
                    nc.vector.tensor_copy(probsT[:, h % 2].rearrange("p j t -> p (j t)"), bank[2 + h % 2][:]
                                          ).then_inc(probsT_ready.sem, 1)

                keep_probsT(0)
                keep_probsT(1)
                splits(58)
                keep_probsT(2)
                keep_probsT(3)
                splits(60)
                dve.wait_ge(*pv_done.at(l, 4))
                dve.wait_ge(*gate0_ready.at(l, MT))
                dve.wait_ge(*inv_ready.at(l, 1))

                def gated(b, y, m, scales, ready):
                    for h in range(HEADS):
                        at = slice(h * HD, (h + 1) * HD)
                        nc.vector.scalar_tensor_tensor(
                            out=y[:, m, at], in0=bank[b][:, at], scalar=scales[:, m * HEADS + h:m * HEADS + h + 1],
                            in1=y[:, m, at], op0=ALU.mult, op1=ALU.mult).then_inc(ready.sem, 1)

                for m in range(MT):
                    gated(m, gate0, m, p_inv, yD_ready)
                splits(63)
                lo_tiles(yTD_rounded, yTD_ready, yT_hi, yT_lo, 2, G_Y + SLOT["D"], slot0=SLOT["D"])
                splits(64)
                dve.wait_ge(*gate1_ready.at(l, MT))
                for m in range(MT):
                    dve.wait_ge(*cm_filled.at(l, m + 1))
                    nc.vector.tensor_tensor(gate1[:, m, :], bank[2 + m][:], gate1[:, m, :], ALU.mult
                                            ).then_inc(yC_ready.sem, 1)
                splits(67)
                lo_tiles(yTC_rounded, yTC_ready, yT_hi, yT_lo, 0, G_Y + SLOT["C"], slot0=SLOT["C"])
                splits(70)
                for m in range(MT):
                    dve.wait_ge(*soft_ready.at(l, m + 1))
                    nc.vector.scalar_tensor_tensor(out=la[:, m, :], in0=bank[2 + m][:], scalar=0.0, in1=la[:, m, :],
                                                   op0=ALU.min, op1=ALU.subtract).then_inc(la_ready.sem, 1)
                splits(76)
                dve.wait_ge(*tb_filled.at(l, 1))
                dve.wait_ge(*e_ready.at(l, 4))
                for d in range(2):
                    splits(76 + d)
                    for i in range(2):
                        rows = slice(64 * i, 64 * i + 64)
                        nc.vector.scalar_tensor_tensor(
                            out=q_heads[rows, d, :, :, i, :].rearrange("p f m t -> p (f m) t"),
                            in0=bank[0][rows, :].rearrange("p (n t) -> p n t", t=P),
                            scalar=GLA_DK ** -0.5,
                            in1=e_pos[rows, d].rearrange("p f (m t) -> p (f m) t", m=MT), op0=ALU.mult, op1=ALU.mult
                            ).then_inc(q_b_ready.sem, 1)
                splits(78)
                dve.wait_ge(*tb_filled.at(l, 2))
                for d in range(2):
                    nc.vector.tensor_tensor(e_neg[:, d].rearrange("p f t -> p (f t)"), bank[1][:],
                                            e_neg[:, d].rearrange("p f t -> p (f t)"), ALU.mult
                                            ).then_inc(k_b_ready.sem, 1)

                def decay_k(m):
                    for c in range(2):
                        rows = slice(64 * c, 64 * c + 64)
                        nc.vector.tensor_tensor(
                            k_dec[rows, :, :, 64 * c:64 * c + 64],
                            bcast(zb[rows, m, 1:2, :].rearrange("p o (h k) -> p o h k", h=HEADS), 1, 2),
                            e_rem[rows, m].rearrange("p d (h k) -> p d h k", h=HEADS), ALU.mult
                            ).then_inc(k_dec_ready.sem, 1)

                splits(79)
                dve.wait_ge(*e_rem_ready.at(l, 2))
                dve.wait_ge(cleared.sem, 5)
                decay_k(0)

                dve.wait_ge(*bits_ready.at(l, 2))

                def pick(m):
                    for d, dst in enumerate((score_b[:, m], picked)):
                        dve.wait_ge(*sb_filled.at(l, 2 * m + d + 1))
                        if m == 1 and d == 1:
                            dve.wait_ge(*score_b_ready.at(l, 1))
                        nc.vector.tensor_tensor(
                            dst.bitcast(I32), bank[(2 + 2 * m + d) % 4][:].rearrange("p (h i) -> p h i", h=HEADS).bitcast(I32),
                            bcast(keep_bits[:, d:d + 1, :], 1, HEADS), ALU.bitwise_and).then_inc(picked_ready.sem, 1)
                    dve.wait_ge(*picked_ready.at(l, 2 * m + 2))
                    nc.vector.tensor_tensor(score_b[:, m], score_b[:, m], picked[:], ALU.add
                                            ).then_inc(score_b_ready.sem, 1)

                splits(80)
                pick(0)
                splits(81)
                pick(1)
                splits(82)
                dve.wait_ge(*kv_filled.at(l, 2))
                decay_k(1)
                splits(84)
                dve.wait_ge(*kv_kept.at(l, 12))
                for t in (1, 2):
                    for d in range(2):
                        edge = GLA_CHUNK * (t + 1) - 1 if d == 0 else GLA_CHUNK * (3 - t)
                        for a in range(2):
                            if t == 2:
                                dve.wait_ge(*state_ready.at(l, 2 * d + a + 1))
                            nc.vector.scalar_tensor_tensor(
                                out=state[:, d, t, a, :], in0=state[:, d, t - 1, a, :],
                                scalar=e_pos[:, d, a, edge:edge + 1], in1=state[:, d, t, a, :],
                                op0=ALU.mult, op1=ALU.add).then_inc(state_ready.sem, 1)

                def head_squares(sq, m, squared, read):
                    dve.wait_ge(*squared.at(l, m + 1))
                    nc.vector.tensor_reduce(o_sq[:, m * HEADS:(m + 1) * HEADS], sq.rearrange("p (h c) -> p h c", h=HEADS),
                                            AX_X, ALU.add).then_inc(read.sem, 1)

                splits(87)
                for m in range(MT):
                    head_squares(sq_b, m, ob_squared, ob_sq_read)
                dve.wait_ge(*ob_sq_read.at(l, 2))
                mean_square(o_sq, o_ms, HD, ob_ms_ready)

                def turn_heads(z, z_ready, rot, turned, at):
                    splits(at)
                    hh = HD // 2
                    dve.wait_ge(*z_ready.at(l, MT))
                    zz = z[:].rearrange("p m (n c) -> p m n c", c=hh)
                    rr = rot[:].rearrange("p (m h) (a c) -> p m (h a) c", m=MT, a=2)

                    def tab(name, n):
                        return bcast(const(name).rearrange("p (m o c) -> p m o c", m=MT, o=1), 2, n)

                    chained(nc.vector.tensor_tensor(rr, zz, tab("rcos", 2 * HEADS), ALU.mult))
                    za = z[:].rearrange("p m (h a c) -> p m h a c", h=HEADS, a=2)
                    ta = rot_a[:].rearrange("p (m h) (a c) -> p m h a c", m=MT, a=2)
                    ra = rot[:].rearrange("p (m h) (a c) -> p (m h) a c", m=MT, a=2)
                    tb = rot_a[:].rearrange("p (m h) (a c) -> p (m h) a c", m=MT, a=2)
                    splits(at + 1)
                    for a in range(2):
                        chained(nc.vector.tensor_tensor(ta[:, :, :, a, :], za[:, :, :, 1 - a, :], tab("rsin", HEADS),
                                                        ALU.mult))
                    splits(at + 2)
                    for a, op in enumerate((ALU.subtract, ALU.add)):
                        nc.vector.tensor_tensor(ra[:, :, a, :], ra[:, :, a, :], tb[:, :, a, :], op
                                                ).then_inc(turned.sem, 1)

                splits(88)
                dve.wait_ge(*ob_rs_ready.at(l, 1))
                dve.wait_ge(*gate0_ready.at(l, 2 * MT))
                for m in range(MT):
                    gated(m, gate0, m, o_rs, yB_ready)
                turn_heads(gate1, z_rq_ready, rq_rot, rq_turned, 89)
                lo_tiles(yTB_rounded, yTB_ready, yT_hi, yT_lo, 2, G_Y + SLOT["B"], slot0=SLOT["B"])
                dve.wait_ge(*rq_turned.at(l, 2))
                turn_heads(z_rk, z_rk_ready, rk_rot, rk_turned, 92)
                splits(100)
                decay = const("decay").rearrange("p (h k i) -> p h k i", h=HEADS, k=3)
                for h in range(HEADS):
                    dve.wait_ge(*sa_filled.at(l, h + 1))
                    tiles = bank[h][:].rearrange("p (j i) -> p j i", j=4)
                    dst = score_a[:, h].rearrange("p j (m i) -> p (j m) i", m=MT)
                    chained(nc.vector.tensor_tensor(dst[:, 0:4:3], tiles[:, 0:4:3], bcast(decay[:, h, 0:1], 1, 2),
                                                    ALU.mult))
                    nc.vector.tensor_tensor(dst[:, 1:3], tiles[:, 1:3], decay[:, h, 1:3], ALU.mult
                                            ).then_inc(score_a_ready.sem, 1)
                splits(104)
                for m in range(MT):
                    head_squares(sq_a, m, oa_squared, oa_sq_read)
                dve.wait_ge(*oa_sq_read.at(l, 2))
                mean_square(o_sq, o_ms, HD, oa_ms_ready)
                splits(107)
                dve.wait_ge(*oa_rs_ready.at(l, 1))
                dve.wait_ge(*gate1_ready.at(l, 2 * MT))
                for m in range(MT):
                    gated(m, gate1, m, o_rs, yA_ready)
                splits(111)
                lo_tiles(yTA_rounded, yTA_ready, yT_hi, yT_lo, 2, G_Y + SLOT["A"], slot0=SLOT["A"])
                dve.wait_ge(*yTA_ready.at(l, 4))
                nc.vector.tensor_copy(gains[:], gains_all[:, bass.ds((l + 1) * GAIN_W, GAIN_W)]
                                      ).then_inc(gains_ready.sem, 1)
                for c in range(4):
                    splits(min(114 + 8 * c, GRANULES))
                    j = END[f"out{c}"] - 1
                    dve.wait_ge(*half_out.at(l, c + 1))
                    for m in range(MT):
                        if m == 1:
                            dve.wait_ge(*multiplied[j % RING].at(l, j // RING + 1))
                        at = x[:, m, c * 512:(c + 1) * 512]
                        nc.vector.tensor_tensor(at, pair[PAIR[f"out{c}"]][m][:], at, ALU.add
                                                ).then_inc(added[c].sem, 1)
                    dve.wait_ge(*added[c].at(l, MT))
                    for m in range(MT):
                        dve.sem_inc(taken[PAIR[f"out{c}"]].sem, 1)
                assert step[0] == dve_step.per_layer, step[0]

        @block.gpsimd
        def _(pool):
            pool.memset(minus_half, -0.5).then_inc(cleared.sem, 1)
            pool.memset(aT[:], 0.0).then_inc(cleared.sem, 1)
            pool.memset(q_heads[:], 0.0).then_inc(cleared.sem, 1)
            pool.memset(k_dec[:], 0.0).then_inc(cleared.sem, 1)
            pool.wait_ge(cleared.sem, 4)
            pool.memset(aT[64:65, :, :], 1.0).then_inc(cleared.sem, 1)

            for c in range(2, 4):
                pool.dma_start(x[:, :, c * 512:(c + 1) * 512],
                               x_in.rearrange("(m p) (c n) -> c p m n", p=P, c=4)[c]).then_inc(x_loaded[c].sem, 16)
            pool.dma_start(consts[:, P:], consts_in[:, P:]).then_inc(consts_loaded.sem, 16)

            with pool.Fori(0, DEPTH) as l:
                def rsqrt(ms, rs, ms_ready, rs_ready):
                    pool.wait_ge(*ms_ready.at(l, 1))
                    n = ms.shape[1]
                    pool.tensor_tensor(rs, ms, minus_half[:, 0:n], ALU.pow).then_inc(rs_ready.sem, 1)

                pool.wait_ge(cleared.sem, 5)
                for j in range(POOL_SPLITS):
                    pool.wait_ge(*rounded[j].at(l, 1))
                    pool.tensor_tensor(lo[j][:], raw[j][:], hi[j][:].bitcast(F32), ALU.subtract
                                       ).then_inc(split[j].sem, 1)
                pool.wait_ge(consts_loaded.sem, 16)
                rsqrt(x_ms, x_rs, x_ms_ready, x_rs_ready)
                pool.wait_ge(*mats_loaded.at(l, 16))
                half = ROPE // 2
                mcos, msin, mnsin = (const(n).rearrange("p (m c) -> p m c", m=MT) for n in ("mcos", "msin", "mnsin"))
                for w in range(2):
                    g = mats[:, M_ROPE + w * ROPE:M_ROPE + (w + 1) * ROPE]
                    g0 = bcast(g[:, 0:half].rearrange("p (o c) -> p o c", o=1), 1, MT)
                    g1 = bcast(g[:, half:].rearrange("p (o c) -> p o c", o=1), 1, MT)
                    gm = bcast(g.rearrange("p (o a c) -> p o a c", o=1, a=2), 1, MT)
                    cm = bcast(mcos.rearrange("p m (o c) -> p m o c", o=1), 2, 2)
                    pool.tensor_tensor(rope_tab[:, w, 0].rearrange("p m (a c) -> p m a c", a=2), gm, cm, ALU.mult
                                       ).then_inc(tabs_ready.sem, 1)
                    pool.tensor_tensor(rope_tab[:, w, 1, :, 0:half], g1, mnsin, ALU.mult).then_inc(tabs_ready.sem, 1)
                    pool.tensor_tensor(rope_tab[:, w, 1, :, half:], g0, msin, ALU.mult).then_inc(tabs_ready.sem, 1)
                rsqrt(lq_ms, lq_rs, lq_ms_ready, lq_rs_ready)
                rsqrt(lk_ms, lk_rs, lk_ms_ready, lk_rs_ready)
                rsqrt(q_ms, q_rs, q_ms_ready, q_rs_ready)
                rsqrt(k_ms, k_rs, k_ms_ready, k_rs_ready)
                rsqrt(o_ms, o_rs, ob_ms_ready, ob_rs_ready)
                rsqrt(o_ms, o_rs, oa_ms_ready, oa_rs_ready)


def shape_constants():
    import numpy as np

    c = np.zeros((P, CONST_W), np.float64)

    def put(name, value):
        at, w = CONSTS[name]
        c[:, at:at + w] = np.asarray(value, np.float64).reshape(P, w)

    i = np.arange(P)
    k, t = i[:, None], i[None, :]
    same = (k // GLA_CHUNK) == (t // GLA_CHUNK)
    put("ident", k == t)
    put("tri_f", same & (k <= t))
    put("tri_b", same & (k >= t))
    put("after", same & (k > t))
    put("before", same & (k < t))
    gamma = 1.0 - 2.0 ** (-5.0 - np.arange(HEADS))
    decay = np.zeros((P, HEADS, 3, P))
    for h in range(HEADS):
        f, b = gamma[h], gamma[HEADS - 1 - h]
        decay[:, h, 0] = np.where(t >= k, f ** (1.0 * np.abs(t - k)), 0) + np.where(k >= t, b ** (1.0 * np.abs(t - k)), 0)
        decay[:, h, 1] = f ** (t + P - k)
        decay[:, h, 2] = b ** (k + P - t)
    put("decay", decay * HD ** -0.5)

    def angles(dim):
        inv = (1.0 / (np.float32(10000.0) ** (np.arange(0, dim, 2, dtype=np.float32) / np.float32(dim)))).astype(np.float32)
        a = (np.arange(SEQ, dtype=np.float32)[:, None] * inv[None, :]).astype(np.float64)
        return a.reshape(MT, P, dim // 2).transpose(1, 0, 2)

    put("rcos", np.cos(angles(HD)))
    put("rsin", np.sin(angles(HD)))
    put("mcos", np.cos(angles(ROPE)))
    put("msin", np.sin(angles(ROPE)))
    put("mnsin", -np.sin(angles(ROPE)))
    band = np.zeros((4, SEQ, SEQ))
    for g, w in enumerate(POOL_WINDOWS):
        for tt in range(SEQ):
            a, b = max(tt - w // 2, 0), min(tt + w // 2, SEQ)
            band[g, a:b, tt] = 1.0 / (b - a)
            band[g, tt, tt] -= 1.0
    cut = np.zeros((P, 4, MT, POOL_REACH))
    cut[:, :, 0] = band[:, 0:P, 0:POOL_REACH].transpose(1, 0, 2)
    cut[:, :, 1] = band[:, P:, SEQ - POOL_REACH:].transpose(1, 0, 2)
    put("band", cut)
    return c.astype(np.float32)


def lay_out(a):
    import numpy as np

    widths = (512, 512, 512, 512, 256, 256, 512, 512, 16, 16, 512, 512, 512, 256, 64, 512)
    names = ("rq", "rk", "rv", "rg", "gq", "gk", "gv", "gg", "af", "ab", "pv", "pg", "mq", "mkv", "mkr", "mg")
    at = dict(zip(names, np.cumsum((0,) + widths[:-1])))
    wide = dict(zip(names, widths))
    parts = {"lat": ("mkv", "af", "ab", "mkr"), "gqk": ("gq", "gk")}
    y_rows = [g * GROUP_W for g in (3, 2, 1, 0)]
    stream = np.zeros((DEPTH, GRANULES, P, 2, 512), np.float32)
    for l in range(DEPTH):
        for name, (width, src, base, n_slots, per) in STAGES.items():
            if name.startswith("out"):
                c = int(name[3:])
                w = np.concatenate([a["w_out"][l, r:r + GROUP_W, c * 512:(c + 1) * 512] for r in y_rows])
            elif name.startswith("wq"):
                w = a["mla_wq_b"][l][:, int(name[2:]) * width:(int(name[2:]) + 1) * width]
            elif name.startswith("wkv"):
                w = a["mla_wkv_b"][l][:, int(name[3:]) * width:(int(name[3:]) + 1) * width]
            else:
                w = np.concatenate([a["w_in"][l][:, at[n]:at[n] + wide[n]] for n in parts.get(name, (name,))], axis=1)
            w = w.reshape(n_slots // per, per, P, width).transpose(0, 2, 1, 3)
            stream[l, [j for j in range(GRANULES) if PLAN[j][0] == name], :, 0:per, 0:width] = w
    stream = stream.reshape(DEPTH, PER_RING, RING, P, GRAN)

    def columns(v):
        return v.reshape(-1, P).T

    gains = np.zeros((P, DEPTH + 1, GAIN_W), np.float32)
    mats = np.zeros((DEPTH, P, MAT_W), np.float32)
    for l in range(DEPTH):
        gains[:, l] = np.concatenate([
            columns(a["norm_g"][l]), np.ones((P, GT), np.float32), columns(a["pool_scale"][l]),
            columns(a["gla_norm_g"][l]), columns(a["ret_norm_g"][l]), columns(a["mla_q_norm_g"][l]),
            columns(a["mla_kv_norm_g"][l]), columns(a["mla_qk_norm_q"][l][:NOPE]),
            columns(a["mla_qk_norm_k"][l][:NOPE])], axis=1)
        mats[l, :, M_POOL:M_POOL + GROUP_W] = a["pool_w"][l].transpose(1, 0, 2).reshape(P, GROUP_W)
        for d, way in enumerate(("f", "b")):
            to = slice(M_WA + d * 256, M_WA + (d + 1) * 256)
            row = WA_ROW + d * GLA_RANK
            mats[l, row:row + GLA_RANK, to] = a[f"gla_wa2_{way}"][l]
            mats[l, WA_ROW + 2 * GLA_RANK, to] = a[f"gla_ba_{way}"][l]
        mats[l, :, M_ROPE:M_ROPE + ROPE] = a["mla_qk_norm_q"][l][NOPE:]
        mats[l, :, M_ROPE + ROPE:] = a["mla_qk_norm_k"][l][NOPE:]
    return {"x_in": a["x"].reshape(SEQ, D_MODEL), "stream": stream, "mats_in": mats,
            "gains_in": gains.reshape(P, (DEPTH + 1) * GAIN_W), "consts_in": shape_constants()}


def kernel(**inputs):
    import numpy as np
    import concourse.bacc as bacc
    from concourse.bass_utils import run_bass_kernel_spmd

    arrays = lay_out({n: np.asarray(v) for n, v in inputs.items()})
    arrays = {n: np.ascontiguousarray(v) for n, v in arrays.items()}
    nc = bacc.Bacc("TRN2", target_bir_lowering=False, num_devices=1)
    args = [nc.dram_tensor(n, v.shape, F32, kind="ExternalInput").ap() for n, v in arrays.items()]
    out = nc.dram_tensor("out", (SEQ, D_MODEL), F32, kind="ExternalOutput").ap()
    build(nc, *args, out)
    result = run_bass_kernel_spmd(nc, [arrays], core_ids=[0])
    return result.results[0]["out"].reshape(1, SEQ, D_MODEL)
```
